# Optimizing a Trainium2 kernel written in Bass

```python
import math
import jax
import jax.numpy as jnp
from jax import lax
import numpy as np

D_MODEL = 1024
BATCH = 1
SEQ = 256
DEPTH = 2

N_EVEN = (DEPTH + 1) // 2
N_ODD = DEPTH // 2
NORM_EPS = 1e-6
HEAD_DIM = 64
ROPE_DIM = HEAD_DIM // 4
ROPE_THETA = 500000.0
MASK_NEG = -1e30

RWKV_HEADS = 8
RWKV_WIDTH = RWKV_HEADS * HEAD_DIM
RWKV_DECAY_RANK = 32
RWKV_A_RANK = 32
RWKV_GATE_RANK = 96
RWKV_GN_EPS = 64e-5
RWKV_COLS = 3 * RWKV_WIDTH + RWKV_DECAY_RANK + RWKV_A_RANK + RWKV_GATE_RANK
RWKV_SPLITS = [RWKV_WIDTH, 2 * RWKV_WIDTH, 3 * RWKV_WIDTH, 3 * RWKV_WIDTH + RWKV_DECAY_RANK, 3 * RWKV_WIDTH + RWKV_DECAY_RANK + RWKV_A_RANK]

NSA_Q_HEADS = 8
NSA_KV_HEADS = 2
NSA_GROUP = NSA_Q_HEADS // NSA_KV_HEADS
NSA_WIDTH = NSA_Q_HEADS * HEAD_DIM
NSA_KV_WIDTH = NSA_KV_HEADS * HEAD_DIM
NSA_COLS = NSA_WIDTH + 6 * NSA_KV_WIDTH + 3 * NSA_Q_HEADS
NSA_SPLITS = [NSA_WIDTH + i * NSA_KV_WIDTH for i in range(7)]
CMP_BLOCK = 32
CMP_STRIDE = 16
CMP_HIDDEN = 2 * HEAD_DIM
SLC_BLOCK = 64
SLC_TOPN = 16
SLC_Q_CHUNK = 64
WINDOW = 512
WIN_BLOCK = 128
FORCED_SCORE = 1e6

HYB_COLS = RWKV_COLS + NSA_COLS
MIX_WIDTH = RWKV_WIDTH + NSA_WIDTH

SSM_D_INNER = 2 * D_MODEL
SSM_HEAD_DIM = 64
SSM_HEADS = SSM_D_INNER // SSM_HEAD_DIM
SSM_GROUPS = 4
SSM_STATE = 128
SSM_CONV = 4
SSM_CHUNK = 256
SSM_NORM_EPS = 1e-5
SSM_CONV_CH = SSM_D_INNER + 2 * SSM_GROUPS * SSM_STATE
SSM_IN_COLS = SSM_D_INNER + SSM_CONV_CH + SSM_HEADS

MOE_GROUPS = 4
MOE_EPG = 8
MOE_EXPERTS = MOE_GROUPS * MOE_EPG
MOE_TOPK = 2
MOE_HIDDEN = 512

kernel_name = 'hybrid_rwkv7_nsa_mamba2_hmoe'

def rms_norm(x, g, eps=NORM_EPS):
    xf = x.astype(jnp.float32)
    y = xf * lax.rsqrt(jnp.mean(xf * xf, -1, keepdims=True) + eps)
    return (y * g.astype(jnp.float32)).astype(x.dtype)

def partial_rope(x, pos):
    half = ROPE_DIM // 2
    inv = jnp.power(ROPE_THETA, -jnp.arange(half, dtype=jnp.float32) * (2.0 / ROPE_DIM))
    ang = pos.astype(jnp.float32)[:, None] * inv[None, :]
    cos = jnp.cos(ang)[:, None, :]
    sin = jnp.sin(ang)[:, None, :]
    xr = x[..., :ROPE_DIM].astype(jnp.float32)
    x1, x2 = xr[..., :half], xr[..., half:]
    rot = jnp.concatenate([x1 * cos - x2 * sin, x2 * cos + x1 * sin], -1).astype(x.dtype)
    return jnp.concatenate([rot, x[..., ROPE_DIM:]], -1)

def token_shift(z):
    return jnp.pad(z, ((0, 0), (1, 0), (0, 0)))[:, :-1]

def rwkv7_scan(r, w, k, v, a, b):
    f32 = jnp.float32
    xs = tuple(jnp.moveaxis(t.astype(f32), 1, 0) for t in (r, w, k, v, a, b))

    def step(state, inp):
        r_t, w_t, k_t, v_t, a_t, b_t = inp
        sa = jnp.einsum('bhij,bhj->bhi', state, a_t)
        state = state * w_t[:, :, None, :] + sa[..., None] * b_t[:, :, None, :] + v_t[..., None] * k_t[:, :, None, :]
        return state, jnp.einsum('bhij,bhj->bhi', state, r_t)

    b_, _, h_, n_ = r.shape
    s0 = jnp.zeros((b_, h_, n_, n_), f32)
    _, ys = lax.scan(step, s0, xs)
    return jnp.moveaxis(ys, 0, 1)

def rwkv7_mix(cols, mu, w0, w_up, a0, a_up, g_up, k_k, k_a, r_k, gn_w, gn_b):
    b_, s_, _ = cols.shape
    f32 = jnp.float32
    z = cols + (token_shift(cols) - cols) * mu
    r, k, v, w_lo, a_lo, g_lo = jnp.split(z, RWKV_SPLITS, axis=-1)
    w_log = -jax.nn.softplus(-(w0 + jnp.tanh(w_lo) @ w_up).astype(f32)) - 0.5
    a = jax.nn.sigmoid(a0 + a_lo @ a_up)
    g = jax.nn.sigmoid(g_lo) @ g_up
    heads = lambda t: t.reshape(b_, s_, RWKV_HEADS, HEAD_DIM)
    kk = heads(k * k_k).astype(f32)
    kk = kk * lax.rsqrt(jnp.maximum(jnp.sum(kk * kk, -1, keepdims=True), 1e-24))
    k = k * (1.0 + (a - 1.0) * k_a)
    r_h, k_h, v_h, a_h = heads(r), heads(k), heads(v), heads(a)
    decay = jnp.exp(-jnp.exp(heads(w_log)))
    y = rwkv7_scan(r_h, decay, k_h, v_h, -kk, kk * a_h)
    mean = jnp.mean(y, -1, keepdims=True)
    var = jnp.mean(jnp.square(y - mean), -1, keepdims=True)
    y = ((y - mean) * lax.rsqrt(var + RWKV_GN_EPS)).reshape(b_, s_, RWKV_WIDTH)
    y = y * gn_w + gn_b
    bonus = jnp.sum(r_h * k_h * r_k, -1, keepdims=True) * v_h
    y = y.astype(cols.dtype) + bonus.reshape(b_, s_, RWKV_WIDTH)
    return y * g

def nsa_mix(cols, pe_k, w1_k, b1_k, w2_k, pe_v, w1_v, b1_v, w2_v):
    b_, s_, _ = cols.shape
    f32 = jnp.float32
    hk, gq, d = NSA_KV_HEADS, NSA_GROUP, HEAD_DIM
    scale = HEAD_DIM ** -0.5
    q, kc, vc, ks, vs, kw, vw, gates = jnp.split(cols, NSA_SPLITS, axis=-1)
    pos = jnp.arange(s_)
    q = partial_rope(q.reshape(b_, s_, NSA_Q_HEADS, d), pos)
    q = q.reshape(b_, s_, hk, gq, d).transpose(0, 2, 3, 1, 4)
    kv_heads = lambda t: t.reshape(b_, s_, hk, d)

    n_cmp = (s_ - CMP_BLOCK) // CMP_STRIDE + 1
    blk_idx = np.arange(n_cmp)[:, None] * CMP_STRIDE + np.arange(CMP_BLOCK)[None, :]
    cmp_end = jnp.asarray(blk_idx[:, -1])

    def compress(t, pe, w1, b1, w2):
        blocks = kv_heads(t)[:, blk_idx] + pe[:, None, :]
        flat = blocks.transpose(0, 1, 3, 2, 4).reshape(b_, n_cmp, hk, CMP_BLOCK * d)
        return jax.nn.silu(flat @ w1 + b1) @ w2

    k_cmp = partial_rope(compress(kc, pe_k, w1_k, b1_k, w2_k), cmp_end).transpose(0, 2, 1, 3)
    v_cmp = compress(vc, pe_v, w1_v, b1_v, w2_v).transpose(0, 2, 1, 3)
    s_cmp = jnp.einsum('bhgsd,bhcd->bhgsc', q, k_cmp).astype(f32) * scale
    cmask = cmp_end[None, :] <= pos[:, None]
    p_cmp = jax.nn.softmax(jnp.where(cmask, s_cmp, MASK_NEG), -1) * cmask
    o_cmp = jnp.einsum('bhgsc,bhcd->bhgsd', p_cmp.astype(q.dtype), v_cmp)

    n_slc = s_ // SLC_BLOCK
    top_n = min(SLC_TOPN, n_slc)
    overlap = np.any((blk_idx[:, :, None] // SLC_BLOCK) == np.arange(n_slc)[None, None, :], axis=1).astype(np.float32)
    imp = jnp.einsum('bhgsc,cj->bhsj', p_cmp, jnp.asarray(overlap))
    blk = jnp.arange(n_slc)[None, :]
    cur = (pos // SLC_BLOCK)[:, None]
    valid = blk <= cur
    forced = (blk == 0) | (blk == cur) | (blk == cur - 1)
    imp = jnp.where(forced, FORCED_SCORE, jnp.where(valid, imp, -FORCED_SCORE))
    _, sel = lax.top_k(imp, top_n)

    k_slc = partial_rope(kv_heads(ks), pos).transpose(0, 2, 1, 3).reshape(b_, hk, n_slc, SLC_BLOCK, d)
    v_slc = kv_heads(vs).transpose(0, 2, 1, 3).reshape(b_, hk, n_slc, SLC_BLOCK, d)
    n_qc = s_ // SLC_Q_CHUNK
    q_ch = q.reshape(b_, hk, gq, n_qc, SLC_Q_CHUNK, d).transpose(3, 0, 1, 2, 4, 5)
    sel_ch = sel.reshape(b_, hk, n_qc, SLC_Q_CHUNK, top_n).transpose(2, 0, 1, 3, 4)
    pos_ch = pos.reshape(n_qc, SLC_Q_CHUNK)
    gather = jax.vmap(jax.vmap(lambda blocks, ix: blocks[ix]))

    def sel_block(args):
        q_c, ix, t = args
        kg = gather(k_slc, ix)
        vg = gather(v_slc, ix)
        s = jnp.einsum('bhgqd,bhqnld->bhgqnl', q_c, kg).astype(f32) * scale
        tok = ix[..., None] * SLC_BLOCK + jnp.arange(SLC_BLOCK)
        m = (tok <= t[None, None, :, None, None])[:, :, None]
        s = jnp.where(m, s, MASK_NEG)
        p = jax.nn.softmax(s.reshape(s.shape[:4] + (-1,)), -1).reshape(s.shape)
        return jnp.einsum('bhgqnl,bhqnld->bhgqd', p.astype(q_c.dtype), vg)

    o_slc = lax.map(sel_block, (q_ch, sel_ch, pos_ch))
    o_slc = o_slc.transpose(1, 2, 3, 0, 4, 5).reshape(b_, hk, gq, s_, d)

    n_wb = s_ // WIN_BLOCK
    n_back = WINDOW // WIN_BLOCK
    k_win = partial_rope(kv_heads(kw), pos).transpose(0, 2, 1, 3)
    v_win = kv_heads(vw).transpose(0, 2, 1, 3)

    def band(t):
        tp = jnp.pad(t, ((0, 0), (0, 0), (WINDOW, 0), (0, 0))).reshape(b_, hk, n_wb + n_back, WIN_BLOCK, d)
        return jnp.concatenate([tp[:, :, j:j + n_wb] for j in range(n_back + 1)], axis=3)

    kb, vb = band(k_win), band(v_win)
    qb = q.reshape(b_, hk, gq, n_wb, WIN_BLOCK, d)
    s_w = jnp.einsum('bhgiqd,bhikd->bhgiqk', qb, kb).astype(f32) * scale
    tq = jnp.arange(n_wb)[:, None] * WIN_BLOCK + jnp.arange(WIN_BLOCK)[None, :]
    tk = (jnp.arange(n_wb)[:, None] - n_back) * WIN_BLOCK + jnp.arange((n_back + 1) * WIN_BLOCK)[None, :]
    wm = (tk[:, None, :] >= 0) & (tk[:, None, :] <= tq[:, :, None]) & (tq[:, :, None] - tk[:, None, :] < WINDOW)
    p_w = jax.nn.softmax(jnp.where(wm, s_w, MASK_NEG), -1)
    o_win = jnp.einsum('bhgiqk,bhikd->bhgiqd', p_w.astype(q.dtype), vb).reshape(b_, hk, gq, s_, d)

    gate = jax.nn.sigmoid(gates.reshape(b_, s_, NSA_Q_HEADS, 3))
    to_bshd = lambda o: o.transpose(0, 3, 1, 2, 4).reshape(b_, s_, NSA_Q_HEADS, d)
    o = gate[..., 0:1] * to_bshd(o_cmp) + gate[..., 1:2] * to_bshd(o_slc) + gate[..., 2:3] * to_bshd(o_win)
    return o.reshape(b_, s_, NSA_WIDTH)

def segsum(a):
    t_ = a.shape[-1]
    cs = jnp.cumsum(a, -1)
    diff = cs[..., :, None] - cs[..., None, :]
    return jnp.where(jnp.tril(jnp.ones((t_, t_), bool)), diff, -jnp.inf)

def ssd_chunked(x, dt, a_head, bm, cm):
    f32 = jnp.float32
    b_, s_, h_, p_ = x.shape
    pad = (-s_) % SSM_CHUNK
    lc = SSM_CHUNK
    nc = (s_ + pad) // lc
    g_, n_ = SSM_GROUPS, SSM_STATE
    e_ = h_ // g_
    padt = lambda t: jnp.pad(t.astype(f32), ((0, 0), (0, pad)) + ((0, 0),) * (t.ndim - 2))
    xc = padt(x.astype(f32) * dt[..., None]).reshape(b_, nc, lc, g_, e_, p_)
    ad = padt(dt * a_head).reshape(b_, nc, lc, g_, e_).transpose(0, 3, 4, 1, 2)
    bc = padt(bm).reshape(b_, nc, lc, g_, n_)
    cc = padt(cm).reshape(b_, nc, lc, g_, n_)
    a_cs = jnp.cumsum(ad, -1)
    lmat = jnp.exp(segsum(ad))
    cb = jnp.einsum('bclgn,bcsgn->bgcls', cc, bc)
    y_diag = jnp.einsum('bgecls,bcsgep->bclgep', cb[:, :, None] * lmat, xc)
    decay_states = jnp.exp(a_cs[..., -1:] - a_cs).transpose(0, 3, 4, 1, 2)
    states = jnp.einsum('bclgn,bclgep->bcgepn', bc, xc * decay_states[..., None])
    states = jnp.concatenate([jnp.zeros_like(states[:, :1]), states], 1)
    chunk_tot = jnp.pad(a_cs[..., -1], ((0, 0), (0, 0), (0, 0), (1, 0)))
    decay_chunk = jnp.exp(segsum(chunk_tot))
    states = jnp.einsum('bgezc,bcgepn->bzgepn', decay_chunk, states)[:, :-1]
    y_off = jnp.einsum('bclgn,bcgepn->bclgep', cc, states) * jnp.exp(a_cs).transpose(0, 3, 4, 1, 2)[..., None]
    return (y_diag + y_off).reshape(b_, nc * lc, h_, p_)[:, :s_]

def mamba2_mix(u, w_in, conv_w, conv_b, dt_bias, a_log, d_skip, norm_w, w_out):
    b_, s_, _ = u.shape
    f32 = jnp.float32
    zxbcdt = u @ w_in
    z, xbc, dt = jnp.split(zxbcdt, [SSM_D_INNER, SSM_D_INNER + SSM_CONV_CH], axis=-1)
    xbc = lax.conv_general_dilated(xbc, conv_w[:, None, :], window_strides=(1,), padding=[(SSM_CONV - 1, 0)],
                                   dimension_numbers=('NWC', 'WIO', 'NWC'), feature_group_count=SSM_CONV_CH)
    xbc = jax.nn.silu(xbc + conv_b)
    xs, bm, cm = jnp.split(xbc, [SSM_D_INNER, SSM_D_INNER + SSM_GROUPS * SSM_STATE], axis=-1)
    dt = jax.nn.softplus((dt + dt_bias).astype(f32))
    a_head = -jnp.exp(a_log.astype(f32))
    xh = xs.reshape(b_, s_, SSM_HEADS, SSM_HEAD_DIM)
    y = ssd_chunked(xh, dt, a_head,
                    bm.reshape(b_, s_, SSM_GROUPS, SSM_STATE), cm.reshape(b_, s_, SSM_GROUPS, SSM_STATE))
    y = y + xh.astype(f32) * d_skip.astype(f32)[:, None]
    y = y.reshape(b_, s_, SSM_D_INNER) * jax.nn.silu(z.astype(f32))
    yg = y.reshape(b_, s_, SSM_GROUPS, SSM_D_INNER // SSM_GROUPS)
    yg = yg * lax.rsqrt(jnp.mean(yg * yg, -1, keepdims=True) + SSM_NORM_EPS)
    y = yg.reshape(b_, s_, SSM_D_INNER) * norm_w.astype(f32)
    return y.astype(u.dtype) @ w_out

def hier_moe(u, wg, bg, we, be, w_gate, w_up, w_down):
    b_, s_, d_ = u.shape
    f32 = jnp.float32
    t = u.reshape(-1, d_)
    pg = jax.nn.softmax((t @ wg + bg).astype(f32), -1)
    g_val, g_idx = lax.top_k(pg, 1)
    le = (t @ we + be).astype(f32).reshape(-1, MOE_GROUPS, MOE_EPG)
    le_sel = jnp.take_along_axis(le, g_idx[:, :, None], 1)[:, 0]
    pe = jax.nn.softmax(le_sel, -1)
    e_val, e_idx = lax.top_k(pe, MOE_TOPK)
    e_w = e_val / jnp.sum(e_val, -1, keepdims=True) * g_val
    expert_id = g_idx * MOE_EPG + e_idx
    comb = jnp.sum(jax.nn.one_hot(expert_id, MOE_EXPERTS, dtype=f32) * e_w[..., None], 1)
    comb = comb.astype(u.dtype).reshape(-1, MOE_GROUPS, MOE_EPG)
    out = jnp.zeros_like(t)
    for grp in range(MOE_GROUPS):
        sl = slice(grp * MOE_EPG, (grp + 1) * MOE_EPG)
        act = jax.nn.silu(jnp.einsum('td,edf->tef', t, w_gate[sl])) * jnp.einsum('td,edf->tef', t, w_up[sl])
        out = out + jnp.einsum('tef,efd->td', act * comb[:, grp, :, None], w_down[sl])
    return out.reshape(b_, s_, d_)

def setup_inputs(seed: int = 0) -> dict:
    key = jax.random.key(seed)
    keys = iter(jax.random.split(key, 64))
    f32 = jnp.float32

    def nrm(shape, scale):
        return jax.random.normal(next(keys), shape, f32) * scale

    def unif(shape, lo, hi):
        return jax.random.uniform(next(keys), shape, f32, lo, hi)

    ne, no, nl = N_EVEN, N_ODD, DEPTH
    dt0 = jnp.exp(unif((no, SSM_HEADS), math.log(1e-3), math.log(1e-1)))
    return {
        'x': nrm((BATCH, SEQ, D_MODEL), 1.0),
        'norm_mix': 1.0 + nrm((nl, D_MODEL), 0.02),
        'norm_ffn': 1.0 + nrm((nl, D_MODEL), 0.02),
        'norm_final': 1.0 + nrm((D_MODEL,), 0.02),
        'hyb_w_in': nrm((ne, D_MODEL, HYB_COLS), D_MODEL ** -0.5),
        'hyb_w_out': nrm((ne, MIX_WIDTH, D_MODEL), MIX_WIDTH ** -0.5),
        'rwkv_mu': unif((ne, RWKV_COLS), 0.0, 1.0),
        'rwkv_w0': unif((ne, RWKV_WIDTH), -5.0, 0.0),
        'rwkv_w_up': nrm((ne, RWKV_DECAY_RANK, RWKV_WIDTH), 0.1),
        'rwkv_a0': nrm((ne, RWKV_WIDTH), 0.1),
        'rwkv_a_up': nrm((ne, RWKV_A_RANK, RWKV_WIDTH), 0.5 * RWKV_A_RANK ** -0.5),
        'rwkv_g_up': nrm((ne, RWKV_GATE_RANK, RWKV_WIDTH), RWKV_GATE_RANK ** -0.5),
        'rwkv_k_k': 0.85 + nrm((ne, RWKV_WIDTH), 0.05),
        'rwkv_k_a': 1.0 + nrm((ne, RWKV_WIDTH), 0.05),
        'rwkv_r_k': nrm((ne, RWKV_HEADS, HEAD_DIM), 0.1),
        'rwkv_gn_w': 1.0 + nrm((ne, RWKV_WIDTH), 0.02),
        'rwkv_gn_b': nrm((ne, RWKV_WIDTH), 0.02),
        'nsa_pe_k': nrm((ne, CMP_BLOCK, HEAD_DIM), 0.1),
        'nsa_w1_k': nrm((ne, CMP_BLOCK * HEAD_DIM, CMP_HIDDEN), (CMP_BLOCK * HEAD_DIM) ** -0.5),
        'nsa_b1_k': nrm((ne, CMP_HIDDEN), 0.02),
        'nsa_w2_k': nrm((ne, CMP_HIDDEN, HEAD_DIM), CMP_HIDDEN ** -0.5),
        'nsa_pe_v': nrm((ne, CMP_BLOCK, HEAD_DIM), 0.1),
        'nsa_w1_v': nrm((ne, CMP_BLOCK * HEAD_DIM, CMP_HIDDEN), (CMP_BLOCK * HEAD_DIM) ** -0.5),
        'nsa_b1_v': nrm((ne, CMP_HIDDEN), 0.02),
        'nsa_w2_v': nrm((ne, CMP_HIDDEN, HEAD_DIM), CMP_HIDDEN ** -0.5),
        'ssm_w_in': nrm((no, D_MODEL, SSM_IN_COLS), D_MODEL ** -0.5),
        'ssm_conv_w': nrm((no, SSM_CONV, SSM_CONV_CH), 0.5),
        'ssm_conv_b': nrm((no, SSM_CONV_CH), 0.02),
        'ssm_dt_bias': dt0 + jnp.log(-jnp.expm1(-dt0)),
        'ssm_a_log': jnp.log(unif((no, SSM_HEADS), 1.0, 16.0)),
        'ssm_d': 1.0 + nrm((no, SSM_HEADS), 0.1),
        'ssm_norm_w': 1.0 + nrm((no, SSM_D_INNER), 0.02),
        'ssm_w_out': nrm((no, SSM_D_INNER, D_MODEL), SSM_D_INNER ** -0.5),
        'moe_wg': nrm((nl, D_MODEL, MOE_GROUPS), D_MODEL ** -0.5),
        'moe_bg': nrm((nl, MOE_GROUPS), 0.01),
        'moe_we': nrm((nl, D_MODEL, MOE_EXPERTS), D_MODEL ** -0.5),
        'moe_be': nrm((nl, MOE_EXPERTS), 0.01),
        'moe_w_gate': nrm((nl, MOE_EXPERTS, D_MODEL, MOE_HIDDEN), D_MODEL ** -0.5),
        'moe_w_up': nrm((nl, MOE_EXPERTS, D_MODEL, MOE_HIDDEN), D_MODEL ** -0.5),
        'moe_w_down': nrm((nl, MOE_EXPERTS, MOE_HIDDEN, D_MODEL), MOE_HIDDEN ** -0.5),
    }

def reference(x, norm_mix, norm_ffn, norm_final, hyb_w_in, hyb_w_out,
              rwkv_mu, rwkv_w0, rwkv_w_up, rwkv_a0, rwkv_a_up, rwkv_g_up, rwkv_k_k, rwkv_k_a, rwkv_r_k,
              rwkv_gn_w, rwkv_gn_b,
              nsa_pe_k, nsa_w1_k, nsa_b1_k, nsa_w2_k, nsa_pe_v, nsa_w1_v, nsa_b1_v, nsa_w2_v,
              ssm_w_in, ssm_conv_w, ssm_conv_b, ssm_dt_bias, ssm_a_log, ssm_d, ssm_norm_w, ssm_w_out,
              moe_wg, moe_bg, moe_we, moe_be, moe_w_gate, moe_w_up, moe_w_down):
    h = x
    for layer in range(DEPTH):
        u = rms_norm(h, norm_mix[layer])
        i = layer // 2
        if layer % 2 == 0:
            cols = u @ hyb_w_in[i]
            y_rwkv = rwkv7_mix(cols[..., :RWKV_COLS], rwkv_mu[i], rwkv_w0[i], rwkv_w_up[i], rwkv_a0[i],
                               rwkv_a_up[i], rwkv_g_up[i], rwkv_k_k[i], rwkv_k_a[i], rwkv_r_k[i],
                               rwkv_gn_w[i], rwkv_gn_b[i])
            y_nsa = nsa_mix(cols[..., RWKV_COLS:], nsa_pe_k[i], nsa_w1_k[i], nsa_b1_k[i], nsa_w2_k[i],
                            nsa_pe_v[i], nsa_w1_v[i], nsa_b1_v[i], nsa_w2_v[i])
            mix = jnp.concatenate([y_rwkv, y_nsa], -1) @ hyb_w_out[i]
        else:
            mix = mamba2_mix(u, ssm_w_in[i], ssm_conv_w[i], ssm_conv_b[i], ssm_dt_bias[i], ssm_a_log[i],
                             ssm_d[i], ssm_norm_w[i], ssm_w_out[i])
        h = h + mix
        h = h + hier_moe(rms_norm(h, norm_ffn[layer]), moe_wg[layer], moe_bg[layer], moe_we[layer],
                         moe_be[layer], moe_w_gate[layer], moe_w_up[layer], moe_w_down[layer])
    return rms_norm(h, norm_final)


_drawn_inputs = setup_inputs


def setup_inputs(seed=0):
    import zlib

    import numpy as np

    out = dict(_drawn_inputs(seed))
    spreads = {}
    factors = {'norm_final': 23.655,
     'nsa_pe_k': 2.938,
     'nsa_b1_k': 64.0,
     'ssm_norm_w': 22.112,
     'moe_bg': 3.435,
     'nsa_b1_v': 3.215,
     'rwkv_gn_b': 3.029,
     'moe_be': 3.328}
    for name, (base, spread) in spreads.items():
        noise = np.random.default_rng([zlib.crc32(name.encode()), seed]).standard_normal(out[name].shape)
        drawn = base * np.exp(spread * noise) if base else spread * noise
        out[name] = jnp.asarray(drawn.astype(out[name].dtype))
    for name, factor in factors.items():
        out[name] = (out[name] * factor).astype(out[name].dtype)
    return out
```

```python
import math
import numpy as np
import concourse.bass as bass
from concourse import mybir
from contextlib import ExitStack

F32 = mybir.dt.float32
F32R = mybir.dt.float32r
U32 = mybir.dt.uint32
I32 = mybir.dt.int32
ALU = mybir.AluOpType
ACT = mybir.ActivationFunctionType
AX = mybir.AxisListType

P = 128
D = 1024
SEQ = 256
HALVES = SEQ // P
KD = D // P
BANK = 512
NEG = -1e30

HEADS, HD = 8, 64
RW = HEADS * HD
W_RANK, A_RANK, G_RANK = 32, 32, 96
RWKV_COLS = 3 * RW + W_RANK + A_RANK + G_RANK
KV = 2
GQ = HEADS // KV
NQ, NKC, NVC, NKS, NVS, NKW, NVW, NGATE = 0, 512, 640, 768, 896, 1024, 1152, 1280
NSA_COLS = 1304
HYB_COLS = RWKV_COLS + NSA_COLS
ROPE_HALF = 8
NCMP, CBLK, CSTR = 15, 32, 16
GN_EPS = 64e-5

DI = 2048
MH = 32
GROUPS = 4
NST = 128
XBC = DI + 2 * GROUPS * NST
SSM_COLS = DI + XBC + MH
NXT = XBC // P

EXPERTS, EG, EPG, FH = 32, 4, 8, 512
CAP = 64
DC = 2048
CHUNKS = 6

def columns(spec):
    at, out = 0, {}
    for name, n in spec:
        out[name] = (at, n)
        at += n
    return out, at


CONST, NCONST = columns([("ident", 128), ("before", 128), ("upto", 128), ("after", 128), ("ones", 128),
                         ("headones", 128), ("fold", 64), ("slots", 128), ("scankeep", 256),
                         ("causal", 256), ("cmpok", 30), ("cos", 16), ("sin", 16), ("ccos", 8), ("csin", 8),
                         ("lev", 7 * 128), ("levT", 7 * 128)])
FEAT, NFEAT = columns([("mu", 12), ("mu_w", 1), ("mu_a", 1), ("mu_g", 1), ("w0", 4), ("a0", 4), ("k_k", 4),
                       ("k_a", 4), ("r_k", 4), ("b1_k", 1), ("b1_v", 1), ("conv_w", 4 * NXT), ("conv_b", NXT)])
ROWS, NROWS = columns([("mix0", D), ("ffn0", D), ("mix1", D), ("ffn1", D), ("final", D), ("gn_w", RW),
                       ("gn_b", RW), ("dt_bias", MH), ("a_log", MH), ("d", MH), ("rb0", 36), ("rb1", 36),
                       ("ssm_norm", DI)])


def shape_tables():
    c = np.zeros((P, NCONST), np.float32)

    def put(name, v):
        at, n = CONST[name]
        c[:, at:at + n] = v.reshape(P, n)

    i = np.arange(P)
    put("ident", np.eye(P))
    put("before", (i[:, None] < i[None, :]).astype(np.float32))
    put("upto", (i[:, None] <= i[None, :]).astype(np.float32))
    put("after", (i[:, None] > i[None, :]).astype(np.float32))
    put("ones", np.ones((P, P)))
    put("headones", (i[:, None] // HD == i[None, :] // HD).astype(np.float32))
    put("fold", (i[:, None] % CAP == np.arange(CAP)[None, :]).astype(np.float32))
    put("slots", np.tile(np.arange(P) % CAP, (P, 1)))
    put("scankeep", np.tile((np.arange(SEQ) % P != 0), (P, 1)))
    put("causal", np.concatenate([np.zeros((P, P)), np.where(i[None, :] <= i[:, None], 0, NEG)], 1))
    tok = i[:, None] + P * np.arange(HALVES)[None, :]
    end = np.arange(NCMP) * CSTR + CBLK - 1
    put("cmpok", (end[None, None, :] <= tok[:, :, None]).astype(np.float32))
    inv = np.power(np.float32(500000.0), -np.arange(ROPE_HALF, dtype=np.float32) * np.float32(2.0 / 16))
    ang = tok[:, :, None].astype(np.float32) * inv
    put("cos", np.cos(ang)), put("sin", np.sin(ang))
    cang = np.zeros((P, ROPE_HALF), np.float32)
    cang[:NCMP] = end[:, None].astype(np.float32) * inv
    put("ccos", np.cos(cang)), put("csin", np.sin(cang))
    lev = np.stack([(i[:, None] >> (l + 1) == i[None, :] >> (l + 1)) & (i[:, None] >> l & 1 == 1)
                    & (i[None, :] >> l & 1 == 0) for l in range(7)], 1).astype(np.float32)
    put("lev", lev), put("levT", np.ascontiguousarray(lev.transpose(2, 1, 0)))
    return c


class Count:

    def __init__(self, key, new):
        self.key, self.n, self.new = key, 0, new

    def one(self, mark=None):
        self.n += 1
        if mark is not None:
            assert mark not in self.new, mark
            self.new[mark] = (self.key, self.n)
        return 1


def build(nc, a, known, new):
    ctx = ExitStack()
    sem = lambda name: ctx.enter_context(nc.semaphore(name))
    pe_done, act_done, dve_done, pool_done = sem("pe_done"), sem("act_done"), sem("dve_done"), sem("pool_done")
    sems = {"pe": pe_done, "act": act_done, "dve": dve_done, "pool": pool_done}
    E = {k: Count(k, new) for k in sems}
    PE, AC, DV, PO = E["pe"], E["act"], E["dve"], E["pool"]

    def at(*mark):
        who, n = known.get(mark, ("pe", 1))
        return sems[who], n

    def sb(stack, name, shape, dt=F32):
        return stack.enter_context(nc.sbuf_tensor(name, shape, dt))

    bank = [ctx.enter_context(nc.psum_tensor(f"bank{i}", [P, BANK], F32)) for i in range(8)]
    h = sb(ctx, "h", [P, HALVES, D])
    cst = sb(ctx, "cst", [P, NCONST])
    feat = sb(ctx, "feat", [P, NFEAT])
    eps_n = sb(ctx, "eps_n", [P, 4])

    def C(name, rows=P):
        o, n = CONST[name]
        return cst[0:rows, o:o + n]

    def FT(name, rows=P):
        o, n = FEAT[name]
        return feat[0:rows, o:o + n]

    def row_src(name):
        o, n = ROWS[name]
        return a["rows"][0:1, o:o + n].to_broadcast([P, n])

    turn = {"n": 0, "at": {}, "last": [None] * 8}

    def take(pe, *job):
        b = turn["n"] % 8
        turn["n"] += 1
        if turn["last"][b] is not None:
            pe.wait_ge(*at("read", *turn["last"][b]))
        turn["last"][b] = job
        new[("bank",) + job] = ("pe", b)
        return bank[b]

    def bank_of(*job):
        return bank[known.get(("bank",) + job, ("pe", 0))[1]]

    def rep(ap, n, axis=1):
        ap = ap.unsqueeze(axis)
        shape = list(ap.shape)
        shape[axis] = n
        return ap.to_broadcast(shape)

    def norm_act(act, tag, junk, ss, rstd):
        for t in range(HALVES):
            act.wait_ge(*at("h", tag, t))
            if t:
                act.wait_ge(act_done, AC.n)
            nc.scalar.activation(junk[:, :], h[:, t, :], ACT.Square, accum_out=ss[:, t:t + 1]).then_inc(
                act_done, AC.one(("ss", tag, t)))
        act.wait_ge(act_done, AC.n)
        nc.scalar.activation(rstd[:, :], ss[:, :], ACT.Sqrt, scale=1.0 / D, bias=eps_n[:, 0:1]).then_inc(
            act_done, AC.one(("std", tag)))

    def norm_dve(dve, tag, rstd, u, gain, gain_sem, gain_n):
        dve.wait_ge(*at("std", tag))
        nc.vector.reciprocal(rstd[:, :], rstd[:, :]).then_inc(dve_done, DV.one())
        dve.wait_ge(gain_sem, gain_n)
        dve.wait_ge(dve_done, DV.n)
        for t in range(HALVES):
            nc.vector.scalar_tensor_tensor(out=u[:, t, :], in0=h[:, t, :], scalar=rstd[:, t:t + 1], in1=gain[:, :],
                                           op0=ALU.mult, op1=ALU.mult).then_inc(dve_done, DV.one(("u", tag, t)))

    def turn_pe(pe, tag, src, tiles, ready):
        for t in range(HALVES):
            pe.wait_ge(*at(*ready, t))
            for q in range(tiles // 4):
                b = take(pe, "turn", tag, t, q)
                for k in range(4):
                    i = nc.tensor.transpose(b[:, k * P:(k + 1) * P], src[:, t, (4 * q + k) * P:(4 * q + k + 1) * P],
                                            C("ident"))
                i.then_inc(pe_done, PE.one(("turn", tag, t, q)))

    def turn_act(act, tag, dst, tiles):
        for t in range(HALVES):
            for q in range(tiles // 4):
                act.wait_ge(*at("turn", tag, t, q))
                nc.scalar.copy(dst[:, 4 * q:4 * q + 4, t * P:(t + 1) * P],
                               bank_of("turn", tag, t, q)[:, :].rearrange("p (k t) -> p k t", k=4)).then_inc(
                    act_done, AC.one(("read", "turn", tag, t, q)))

    s_ld = {n: sem("ld_" + n) for n in ("small", "gain", "w0", "w1", "w2", "par", "out")}
    loads = {n: 0 for n in s_ld}

    def got(name):
        return s_ld[name], loads[name]

    def load(eng, name, dst, src):
        loads[name] += 16
        eng.dma_start(dst, src).then_inc(s_ld[name], 16)

    hyb = ExitStack()
    nsa = sb(hyb, "nsa", [P, HALVES, NSA_COLS])
    mix = sb(hyb, "mix", [P, HALVES, D])
    z = sb(hyb, "z", [P, 12, SEQ + 1])
    zlo = sb(hyb, "zlo", [P, 3, SEQ + 1])
    par = sb(hyb, "par", [P, 3 * RW + 2 * RW])
    proj = ExitStack()
    zz, lo3 = sb(hyb, "zz", [P, 12, SEQ]), sb(hyb, "lo3", [P, 3, SEQ])
    gain = sb(proj, "gain", [P, D])
    junk = sb(proj, "junk", [P, D])
    ss = sb(proj, "ss", [P, HALVES])
    rstd = sb(proj, "rstd", [P, HALVES])
    u = sb(proj, "u", [P, HALVES, D])
    uT = sb(proj, "uT", [P, KD, SEQ])
    wr = sb(proj, "wr", [P, 3, KD, BANK])
    GRP = [(0, 512), (512, 512), (1024, 512), (1536, 160), (1696, 512), (2208, 512), (2720, 280)]
    FJOBS = [(g, j) for g in range(3) for j in range(2)]
    LO = [(0, W_RANK), (W_RANK, A_RANK), (W_RANK + A_RANK, G_RANK)]
    w_hyb = a["hyb_w_in"][0].rearrange("(k p) n -> p k n", p=P)

    with nc.Block(name="hyb_in", no_gpsimd_drain=True) as block:

        @block.sync
        def _(sp):
            load(sp, "small", h[:, :, :], a["x"][0].rearrange("(t p) d -> p t d", p=P))
            load(sp, "small", cst[:, :], a["tables"])
            load(sp, "small", feat[:, :], a["feat"])
            load(sp, "gain", gain[:, :], row_src("mix0"))
            for g, (c0, n) in enumerate(GRP):
                if g >= 3:
                    sp.wait_ge(*at("group", g - 3))
                load(sp, f"w{g % 3}", wr[:, g % 3, :, 0:n], w_hyb[:, :, c0:c0 + n])
            load(sp, "par", par[0:W_RANK, 0:RW], a["rwkv_w_up"][0])
            load(sp, "par", par[0:A_RANK, RW:2 * RW], a["rwkv_a_up"][0])
            load(sp, "par", par[0:G_RANK, 2 * RW:3 * RW], a["rwkv_g_up"][0])
            load(sp, "par", par[:, 3 * RW:4 * RW], row_src("gn_w"))
            load(sp, "par", par[:, 4 * RW:5 * RW], row_src("gn_b"))

        @block.vector
        def _(dve):
            nc.vector.memset(eps_n[:, 0:1], 1e-6)
            nc.vector.memset(eps_n[:, 1:2], GN_EPS)
            nc.vector.memset(eps_n[:, 2:3], 1e-5)
            nc.vector.memset(eps_n[:, 3:4], 0.0)
            nc.vector.memset(z[:, :, 0:1], 0.0)
            nc.vector.memset(zlo[:, :, 0:1], 0.0).then_inc(dve_done, DV.one(("consts",)))
            dve.wait_ge(s_ld["small"], 48)
            norm_dve(dve, "mix0", rstd, u, gain, s_ld["gain"], 16)

            def did(ins, *mark):
                ins.then_inc(dve_done, DV.one(mark or None))
                dve.wait_ge(dve_done, DV.n)

            V = nc.vector
            for g, j in FJOBS:
                dve.wait_ge(*at("read", "feat", g, j))
                c0 = 4 * g + 2 * j
                did(V.tensor_tensor(zz[:, c0:c0 + 2, :], z[:, c0:c0 + 2, 0:SEQ], z[:, c0:c0 + 2, 1:SEQ + 1],
                                    ALU.subtract))
                for c in (c0, c0 + 1):
                    did(V.scalar_tensor_tensor(out=zz[:, c, :], in0=zz[:, c, :], scalar=FT("mu")[:, c:c + 1],
                                               in1=z[:, c, 1:SEQ + 1], op0=ALU.mult, op1=ALU.add), "zz", c)
            for i, (n, mu) in enumerate(((W_RANK, "mu_w"), (A_RANK, "mu_a"), (G_RANK, "mu_g"))):
                dve.wait_ge(*at("read", "lo", i))
                did(V.tensor_tensor(lo3[0:n, i, :], zlo[0:n, i, 0:SEQ], zlo[0:n, i, 1:SEQ + 1], ALU.subtract))
                did(V.scalar_tensor_tensor(out=lo3[0:n, i, :], in0=lo3[0:n, i, :], scalar=FT(mu, n),
                                           in1=zlo[0:n, i, 1:SEQ + 1], op0=ALU.mult, op1=ALU.add), "zlo", i)
            for g in range(4, 7):
                n = GRP[g][1]
                o = GRP[g][0] - RWKV_COLS
                dve.wait_ge(*at("nsa", g, 1))
                nc.vector.tensor_copy(nsa[:, 1, o:o + n], bank_of("nsa", g, 1)[:, 0:n]).then_inc(
                    dve_done, DV.one(("read", "nsa", g, 1)))

        @block.scalar
        def _(act):
            act.wait_ge(s_ld["small"], 48)
            act.wait_ge(*at("consts"))
            nc.scalar.copy(junk[:, 0:1], h[:, 0, 0:1]).then_inc(act_done, AC.one())
            new[("h", "mix0", 0)] = new[("h", "mix0", 1)] = ("act", AC.n)
            norm_act(act, "mix0", junk, ss, rstd)
            turn_act(act, "mix0", uT, KD)
            for g, j in FJOBS:
                act.wait_ge(*at("feat", g, j))
                nc.scalar.copy(z[:, 4 * g + 2 * j:4 * g + 2 * j + 2, 1:SEQ + 1],
                               bank_of("feat", g, j)[:, :].rearrange("p (c t) -> p c t", c=2)).then_inc(
                    act_done, AC.one(("read", "feat", g, j)))
            for i, (c0, n) in enumerate(LO):
                act.wait_ge(*at("lo", i))
                nc.scalar.copy(zlo[0:n, i, 1:SEQ + 1], bank_of("lo", i)[0:n, 0:SEQ]).then_inc(
                    act_done, AC.one(("read", "lo", i)))
            for g in range(4, 7):
                n = GRP[g][1]
                o = GRP[g][0] - RWKV_COLS
                act.wait_ge(*at("nsa", g, 0))
                nc.scalar.copy(nsa[:, 0, o:o + n], bank_of("nsa", g, 0)[:, 0:n]).then_inc(
                    act_done, AC.one(("read", "nsa", g, 0)))

        @block.tensor
        def _(pe):
            pe.wait_ge(s_ld["small"], 48)
            turn_pe(pe, "mix0", u, KD, ("u", "mix0"))
            pe.wait_ge(*at("read", "turn", "mix0", 1, 1))
            for g, (c0, n) in enumerate(GRP):
                pe.wait_ge(s_ld[f"w{g % 3}"], 16 * (g // 3 + 1))
                if g < 3:
                    for j in range(2):
                        b = take(pe, "feat", g, j)
                        for c in range(2):
                            for k in range(KD):
                                i = nc.tensor.matmul(b[:, c * SEQ:(c + 1) * SEQ],
                                                     wr[:, g % 3, k, (2 * j + c) * P:(2 * j + c + 1) * P], uT[:, k, :],
                                                     start=(k == 0), stop=(k == KD - 1))
                        i.then_inc(pe_done, PE.one(("feat", g, j)))
                elif g == 3:
                    for x, (o, m) in enumerate(LO):
                        b = take(pe, "lo", x)
                        for k in range(KD):
                            i = nc.tensor.matmul(b[0:m, 0:SEQ], wr[:, 0, k, o:o + m], uT[:, k, :],
                                                 start=(k == 0), stop=(k == KD - 1))
                        i.then_inc(pe_done, PE.one(("lo", x)))
                else:
                    for t in range(HALVES):
                        b = take(pe, "nsa", g, t)
                        for k in range(KD):
                            i = nc.tensor.matmul(b[:, 0:n], uT[:, k, t * P:(t + 1) * P], wr[:, g % 3, k, 0:n],
                                                 start=(k == 0), stop=(k == KD - 1))
                        i.then_inc(pe_done, PE.one(("nsa", g, t)))
                new[("group", g)] = ("pe", PE.n)
    proj.close()

    rwk = ExitStack()
    R4 = lambda name: sb(rwk, name, [P, 4, SEQ])
    dcy, amt, cum, exc = R4("dcy"), R4("amt"), R4("cum"), R4("exc")
    dd, kk, kk2, kp = R4("dd"), R4("kk"), R4("kk2"), R4("kp")
    bh, kh, rt = R4("bh"), R4("kh"), R4("rt")
    av, rk = kk2, dcy
    gate = sb(rwk, "gate", [P, HALVES, RW])
    vt, bt, kt = (sb(rwk, n, [P, HALVES, RW]) for n in ("vt", "bt", "kt"))
    SL = 2 * HEADS
    NT, NN, AKT, RBT, RKT = (sb(rwk, n, [P, SL, P]) for n in ("NT", "NN", "AKT", "RBT", "RKT"))
    tri, triT, prod = (sb(rwk, n, [P, SL, P]) for n in ("tri", "triT", "prod"))
    bon = sb(rwk, "bon", [P, HALVES, HEADS])
    mid = sb(rwk, "mid", [P, 4, HALVES])
    scl = sb(rwk, "scl", [P, 4])
    st8 = sb(rwk, "st8", [P, 3, HALVES * HEADS])
    rhs1 = sb(rwk, "rhs1", [P, RW])
    uu = dd[:, 0:2, :].rearrange("p c t -> p (c t)")
    S0 = dd[:, 2, :].rearrange("p (c i) -> p c i", i=HD)
    r4, k4, v4 = zz[:, 0:4, :], zz[:, 4:8, :], zz[:, 8:12, :]
    w_up, a_up, g_up = par[0:W_RANK, 0:RW], par[0:A_RANK, RW:2 * RW], par[0:G_RANK, 2 * RW:3 * RW]
    MATS = [("NT", NT, bh, av, "before"), ("NN", NN, av, bh, "after"), ("AKT", AKT, kh, av, "before"),
            ("RBT", RBT, bh, rt, "upto"), ("RKT", RKT, kh, rt, "upto")]
    LEVELS = range(1, 7)

    with nc.Block(name="rwkv", no_gpsimd_drain=True) as block:

        @block.vector
        def _(dve):
            def mine():
                dve.wait_ge(dve_done, DV.n)

            def did(ins, *mark):
                ins.then_inc(dve_done, DV.one(mark or None))
                mine()

            V = nc.vector
            did(V.tensor_tensor(kk[:, :, :], k4, rep(FT("k_k"), SEQ, 2), ALU.mult))
            did(V.tensor_tensor(kk2[:, :, :], kk[:, :, :], kk[:, :, :], ALU.mult), "kk2")
            for j in range(2):
                dve.wait_ge(*at("knorm", j))
                did(V.tensor_scalar(kp[:, 2 * j:2 * j + 2, :],
                                    bank_of("knorm", j)[:, :].rearrange("p (c t) -> p c t", c=2), 1e-24, None,
                                    ALU.max), "read", "knorm", j)
            for c in range(4):
                dve.wait_ge(*at("dcy", c))
            did(V.tensor_scalar(dcy[:, :, :], dcy[:, :, :], -math.exp(-0.5), None, ALU.mult))
            for c in range(4):
                did(V.tensor_tensor_scan(cum[:, c, :], C("scankeep"), dcy[:, c, :], 0.0, ALU.mult, ALU.add))
            cum5 = cum[:, :, :].rearrange("p c (t s) -> p c t s", t=HALVES)
            did(V.tensor_copy(mid[:, :, :], cum5[:, :, :, P // 2 - 1]))
            did(V.tensor_tensor(cum5, cum5, rep(mid[:, :, :], P, 3), ALU.subtract))
            did(V.tensor_tensor(exc[:, :, :], cum[:, :, :], dcy[:, :, :], ALU.subtract))
            did(V.tensor_tensor(scl[:, :], cum5[:, :, 0, P - 1], mid[:, :, 1], ALU.add), "logs")
            dve.wait_ge(*at("ksqrt"))
            did(V.reciprocal(kp[:, :, :], kp[:, :, :]))
            did(V.tensor_tensor(kk[:, :, :], kk[:, :, :], kp[:, :, :], ALU.mult))
            for c in range(4):
                dve.wait_ge(*at("amt", c))
            did(V.scalar_tensor_tensor(out=kp[:, :, :], in0=amt[:, :, :], scalar=-1.0, in1=rep(FT("k_a"), SEQ, 2),
                                       op0=ALU.add, op1=ALU.mult))
            did(V.scalar_tensor_tensor(out=kp[:, :, :], in0=kp[:, :, :], scalar=1.0, in1=k4, op0=ALU.add,
                                       op1=ALU.mult))
            did(V.tensor_tensor(rk[:, :, :], r4, kp[:, :, :], ALU.mult))
            did(V.tensor_tensor(rk[:, :, :], rk[:, :, :], rep(FT("r_k"), SEQ, 2), ALU.mult), "rk")
            dve.wait_ge(*at("exps"))
            did(V.scalar_tensor_tensor(out=av[:, :, :], in0=kk[:, :, :], scalar=-1.0, in1=exc[:, :, :],
                                       op0=ALU.mult, op1=ALU.mult))
            did(V.tensor_tensor(bh[:, :, :], kk[:, :, :], amt[:, :, :], ALU.mult))
            did(V.tensor_tensor(bh[:, :, :], bh[:, :, :], cum[:, :, :], ALU.mult))
            did(V.tensor_tensor(kh[:, :, :], kp[:, :, :], cum[:, :, :], ALU.mult))
            did(V.tensor_tensor(rt[:, :, :], r4, dd[:, :, :], ALU.mult), "hats")
            for name, dst, _, _, mask in MATS:
                for t in range(HALVES):
                    for e in range(2):
                        dve.wait_ge(*at("mat", name, t, e))
                        did(V.tensor_tensor(dst[:, t * 8 + e * 4:t * 8 + e * 4 + 4, :],
                                            bank_of("mat", name, t, e)[:, :].rearrange("p (c s) -> p c s", c=4),
                                            rep(C(mask), 4), ALU.mult), "read", "mat", name, t, e)
                if name == "NN":
                    lev, levT = C("lev"), C("levT")
                    for dst2, src, m in ((tri, NN, lev), (triT, NT, levT)):
                        did(V.tensor_tensor(dst2[:, :, :], src[:, :, :], rep(m[:, 0:P], SL), ALU.mult))
                        did(V.tensor_tensor(dst2[:, :, :], dst2[:, :, :], rep(C("ident"), SL), ALU.add),
                            "tri0", 0 if dst2 is tri else 1)
                    did(V.tensor_tensor(NN[:, :, :], NT[:, :, :], rep(levT[:, P:2 * P], SL), ALU.mult), "lvl", 1)
            for l in LEVELS:
                if l + 1 in LEVELS:
                    dve.wait_ge(*at("prod", l, 3))
                    did(V.tensor_tensor(NN[:, :, :], NT[:, :, :], rep(levT[:, (l + 1) * P:(l + 2) * P], SL),
                                        ALU.mult), "lvl", l + 1)
                for g in range(4):
                    for name, dst in (("dT", tri), ("dTT", triT)):
                        if name == "dT" and l == LEVELS[-1]:
                            continue
                        dve.wait_ge(*at(name, l, g))
                        sl = dst[:, 4 * g:4 * g + 4, :]
                        did(V.tensor_tensor(sl, bank_of(name, l, g)[:, :].rearrange("p (c s) -> p c s", c=4), sl,
                                            ALU.add), "read", name, l, g)
            for t in range(HALVES):
                dve.wait_ge(*at("akv", t))
                V3 = lambda ap: ap.rearrange("p (c e i) -> p e c i", e=2, i=HD)
                if t == 0:
                    did(V.tensor_copy(rhs1[:, :], bank_of("akv", t)[:, :]), "rhs1", t)
                else:
                    did(V.tensor_copy(rhs1[:, :], bank_of("akv", t)[:, :]))
                    for e in range(2):
                        dve.wait_ge(*at("as0", e))
                        did(V.tensor_tensor(V3(rhs1[:, :])[:, e], V3(rhs1[:, :])[:, e],
                                            bank_of("as0", e)[:, 0:256].rearrange("p (c i) -> p c i", c=4),
                                            ALU.add), "read", "as0", e)
                    new[("rhs1", t)] = ("dve", DV.n)
                new[("read", "akv", t)] = ("dve", DV.n)
                dve.wait_ge(*at("uu", t))
                did(V.tensor_copy(uu, bank_of("uu", t)[:, :]), "read", "uu", t)
                dve.wait_ge(*at("y", t))
                did(V.tensor_copy(mix[:, t, 0:RW], bank_of("y", t)[:, :]), "read", "y", t)
                if t == 0:
                    dve.wait_ge(*at("s1"))
                    dve.wait_ge(*at("sclexp"))
                    did(V.tensor_tensor(S0, bank_of("s1")[:, 0:256].rearrange("p (c i) -> p c i", c=4),
                                        rep(scl[:, :], HD, 2), ALU.mult), "read", "s1")
                else:
                    for e in range(2):
                        dve.wait_ge(*at("ys0", e))
                        did(V.tensor_tensor(V3(mix[:, t, 0:RW])[:, e], V3(mix[:, t, 0:RW])[:, e],
                                            bank_of("ys0", e)[:, 0:256].rearrange("p (c i) -> p c i", c=4),
                                            ALU.add), "read", "ys0", e)
            dve.wait_ge(*got("par"))
            Y = mix[:, :, 0:RW].rearrange("p t (n i) -> p t n i", i=HD)
            sums = st8[:, 0, :].rearrange("p (t n) -> p t n", t=HALVES)
            sq = prod[:, 0:8, :].rearrange("p (t a) (b i) -> p t (a b) i", t=HALVES, i=HD)
            did(V.tensor_reduce(sums, Y, AX.X, ALU.add))
            did(V.tensor_scalar(sums, sums, 1.0 / HD, None, ALU.mult))
            for t in range(HALVES):
                did(V.tensor_tensor(Y[:, t], Y[:, t], rep(sums[:, t], HD, 2), ALU.subtract))
            for t in range(HALVES):
                did(V.tensor_tensor(sq[:, t], Y[:, t], Y[:, t], ALU.mult))
            did(V.tensor_reduce(sums, sq, AX.X, ALU.add), "gnsum")
            dve.wait_ge(*at("gnsqrt"))
            did(V.reciprocal(sums, sums))
            for t in range(HALVES):
                dve.wait_ge(*at("read", "bon"))
                dve.wait_ge(*at("read", "gup", t))
                Vt = vt[:, t, :].rearrange("p (n i) -> p n i", i=HD)
                did(V.tensor_tensor(Y[:, t], Y[:, t], rep(sums[:, t], HD, 2), ALU.mult))
                did(V.tensor_tensor(mix[:, t, 0:RW], mix[:, t, 0:RW], par[:, 3 * RW:4 * RW], ALU.mult))
                did(V.tensor_tensor(mix[:, t, 0:RW], mix[:, t, 0:RW], par[:, 4 * RW:5 * RW], ALU.add))
                did(V.tensor_tensor(sq[:, t], Vt, rep(bon[:, t, :], HD, 2), ALU.mult))
                did(V.tensor_tensor(Y[:, t], Y[:, t], sq[:, t], ALU.add))
                did(V.tensor_tensor(mix[:, t, 0:RW], mix[:, t, 0:RW], gate[:, t, :], ALU.mult))

        @block.scalar
        def _(act):
            S = nc.scalar
            act.wait_ge(*at("zlo", 0))
            S.activation(lo3[0:W_RANK, 0, :], lo3[0:W_RANK, 0, :], ACT.Tanh).then_inc(act_done, AC.one(("tanh",)))
            act.wait_ge(*at("zlo", 2))
            S.activation(lo3[0:G_RANK, 2, :], lo3[0:G_RANK, 2, :], ACT.Sigmoid).then_inc(act_done,
                                                                                      AC.one(("sgate",)))
            for name, dst, bias in (("wup", dcy, "w0"), ("aup", amt, "a0")):
                for j in range(2):
                    act.wait_ge(*at(name, j))
                    for c in (2 * j, 2 * j + 1):
                        S.activation(dst[:, c, :], bank_of(name, j)[:, (c % 2) * SEQ:(c % 2 + 1) * SEQ], ACT.Sigmoid,
                                     bias=FT(bias)[:, c:c + 1]).then_inc(
                            act_done, AC.one(("dcy" if dst is dcy else "amt", c)))
                    new[("read", name, j)] = ("act", AC.n)
            for t in range(HALVES):
                act.wait_ge(*at("gup", t))
                S.copy(gate[:, t, :], bank_of("gup", t)[:, :]).then_inc(act_done, AC.one(("read", "gup", t)))
            act.wait_ge(*at("read", "knorm", 1))
            S.activation(kp[:, :, :], kp[:, :, :], ACT.Sqrt).then_inc(act_done, AC.one(("ksqrt",)))
            act.wait_ge(*at("logs"))
            S.activation(dd[:, :, :], cum[:, :, :], ACT.Exp).then_inc(act_done, AC.one())
            S.activation(exc[:, :, :], exc[:, :, :], ACT.Exp).then_inc(act_done, AC.one())
            S.activation(scl[:, :], scl[:, :], ACT.Exp).then_inc(act_done, AC.one(("sclexp",)))
            act.wait_ge(act_done, AC.n)
            S.activation(cum[:, :, :], cum[:, :, :], ACT.Exp, scale=-1.0).then_inc(act_done, AC.one(("exps",)))
            act.wait_ge(*at("bon"))
            S.copy(bon[:, :, :], bank_of("bon")[:, 0:2 * HEADS].rearrange("p (t n) -> p t n", t=2)).then_inc(
                act_done, AC.one(("read", "bon")))
            for name, dst in (("vt", vt), ("bt", bt), ("kt", kt)):
                for t in range(HALVES):
                    act.wait_ge(*at(name, t))
                    S.copy(dst[:, t, :], bank_of(name, t)[:, :]).then_inc(act_done, AC.one(("read", name, t)))
            for l in LEVELS:
                for g in range(4):
                    act.wait_ge(*at("prod", l, g))
                    if l > 1:
                        act.wait_ge(*at("dTT", l - 1, g))
                    S.copy(prod[:, 4 * g:4 * g + 4, :],
                           bank_of("prod", l, g)[:, :].rearrange("p (c s) -> p c s", c=4)).then_inc(
                        act_done, AC.one(("read", "prod", l, g)))
            act.wait_ge(*at("gnsum"))
            S.activation(st8[:, 0, :], st8[:, 0, :], ACT.Sqrt, scale=1.0 / HD, bias=eps_n[:, 1:2]).then_inc(
                act_done, AC.one(("gnsqrt",)))

        @block.tensor
        def _(pe):
            T = nc.tensor
            pe.wait_ge(*at("kk2"))
            for j in range(2):
                b = take(pe, "knorm", j)
                T.matmul(b[:, :], C("headones"), kk2[:, 2 * j:2 * j + 2, :].rearrange("p c t -> p (c t)"),
                         start=True, stop=True).then_inc(pe_done, PE.one(("knorm", j)))
            pe.wait_ge(*got("par"))
            pe.wait_ge(*at("tanh"))
            pe.wait_ge(*at("zlo", 1))
            for name, wt, x, m in (("wup", w_up, 0, W_RANK), ("aup", a_up, 1, A_RANK)):
                for j in range(2):
                    b = take(pe, name, j)
                    for c in (2 * j, 2 * j + 1):
                        i = T.matmul(b[:, (c % 2) * SEQ:(c % 2 + 1) * SEQ], wt[:, c * P:(c + 1) * P], lo3[0:m, x, :],
                                     start=True, stop=True)
                    i.then_inc(pe_done, PE.one((name, j)))
            pe.wait_ge(*at("sgate"))
            for t in range(HALVES):
                b = take(pe, "gup", t)
                T.matmul(b[:, :], lo3[0:G_RANK, 2, t * P:(t + 1) * P], g_up, start=True, stop=True).then_inc(
                    pe_done, PE.one(("gup", t)))
            pe.wait_ge(*at("rk"))
            b = take(pe, "bon")
            for t in range(HALVES):
                for c in range(4):
                    i = T.matmul(b[:, t * HEADS + 2 * c:t * HEADS + 2 * c + 2], rk[:, c, t * P:(t + 1) * P],
                                 C("headones")[:, 0:P:HD], start=True, stop=True)
            i.then_inc(pe_done, PE.one(("bon",)))
            pe.wait_ge(*at("hats"))
            for name, src in (("vt", v4), ("bt", bh), ("kt", kh)):
                for t in range(HALVES):
                    b = take(pe, name, t)
                    for c in range(4):
                        i = T.transpose(b[:, c * P:(c + 1) * P], src[:, c, t * P:(t + 1) * P], C("ident"))
                    i.then_inc(pe_done, PE.one((name, t)))
            for name, _, left, right, _ in MATS:
                for t in range(HALVES):
                    for e in range(2):
                        b = take(pe, "mat", name, t, e)
                        for c in range(4):
                            i = T.matmul(b[:, c * P:(c + 1) * P], left[HD * e:HD * e + HD, c, t * P:(t + 1) * P],
                                         right[HD * e:HD * e + HD, c, t * P:(t + 1) * P], start=True, stop=True)
                        i.then_inc(pe_done, PE.one(("mat", name, t, e)))
            for l in LEVELS:
                pe.wait_ge(*at("lvl", l))
                pe.wait_ge(*at("tri0", 1))
                for g in range(4):
                    if l > 1:
                        pe.wait_ge(*at("read", "dTT", l - 1, g))
                    b = take(pe, "prod", l, g)
                    for s in range(4):
                        i = T.matmul(b[:, s * P:(s + 1) * P], NN[:, 4 * g + s, :], tri[:, 4 * g + s, :],
                                     start=True, stop=True)
                    i.then_inc(pe_done, PE.one(("prod", l, g)))
                for g in range(4):
                    pe.wait_ge(*at("read", "prod", l, g))
                    for name, left, right in (("dT", triT, prod), ("dTT", prod, triT)):
                        if name == "dT" and l == LEVELS[-1]:
                            continue
                        b = take(pe, name, l, g)
                        for s in range(4):
                            i = T.matmul(b[:, s * P:(s + 1) * P], left[:, 4 * g + s, :], right[:, 4 * g + s, :],
                                         start=True, stop=True)
                        i.then_inc(pe_done, PE.one((name, l, g)))
            slot = lambda t, n: t * 8 + (n % 2) * 4 + n // 2
            col = lambda n: slice(n * HD, (n + 1) * HD)
            pe.wait_ge(*at("read", "kt", 1))
            for t in range(HALVES):
                b = take(pe, "akv", t)
                pe.wait_ge(*at("read", "mat", "RKT", 1, 1))
                for n in range(HEADS):
                    i = T.matmul(b[:, col(n)], AKT[:, slot(t, n), :], vt[:, t, col(n)], start=True, stop=True)
                i.then_inc(pe_done, PE.one(("akv", t)))
                if t:
                    pe.wait_ge(*at("read", "s1"))
                    for name, left in (("as0", av), ("ys0", rt)):
                        for e in range(2):
                            b = take(pe, name, e)
                            for c in range(4):
                                i = T.matmul(b[:, c * HD:(c + 1) * HD], left[HD * e:HD * e + HD, c, t * P:(t + 1) * P],
                                             S0[HD * e:HD * e + HD, c, :], start=True, stop=True)
                            i.then_inc(pe_done, PE.one((name, e)))
                b = take(pe, "uu", t)
                pe.wait_ge(*at("rhs1", t))
                pe.wait_ge(*at("read", "dTT", 6, 3))
                for n in range(HEADS):
                    i = T.matmul(b[:, col(n)], triT[:, slot(t, n), :], rhs1[:, col(n)], start=True, stop=True)
                i.then_inc(pe_done, PE.one(("uu", t)))
                pe.wait_ge(*at("read", "uu", t))
                b = take(pe, "y", t)
                for n in range(HEADS):
                    T.matmul(b[:, col(n)], RBT[:, slot(t, n), :], uu[:, col(n)], start=True, stop=False)
                    i = T.matmul(b[:, col(n)], RKT[:, slot(t, n), :], vt[:, t, col(n)], start=False, stop=True)
                i.then_inc(pe_done, PE.one(("y", t)))
                if t == 0:
                    b = take(pe, "s1")
                    for n in range(HEADS):
                        o = b[HD * (n % 2):HD * (n % 2) + HD, (n // 2) * HD:(n // 2 + 1) * HD]
                        T.matmul(o, bt[:, t, col(n)], uu[:, col(n)], start=True, stop=False)
                        i = T.matmul(o, kt[:, t, col(n)], vt[:, t, col(n)], start=False, stop=True)
                    i.then_inc(pe_done, PE.one(("s1",)))
    rwk.close()

    att = ExitStack()
    qT = sb(att, "qT", [HD, HEADS, SEQ])
    kT = sb(att, "kT", [HD, 2, KV, SEQ])
    cT = sb(att, "cT", [HD, 2, KV, SEQ])
    w1 = sb(att, "w1", [HD, 2, CBLK, P])
    w2 = sb(att, "w2", [P, 2, HD])
    pe_ = sb(att, "pe_", [HD, 2, CBLK])
    blk = sb(att, "blk", [HD, CBLK, 2 * NCMP])
    blk2 = sb(att, "blk2", [HD, CBLK, 2 * NCMP])
    hid = sb(att, "hid", [P, 2, 2 * NCMP])
    hsg = sb(att, "hsg", [P, 2, 2 * NCMP])
    cmp_ = sb(att, "cmp_", [NCMP, 2, KV, HD])
    kcT = sb(att, "kcT", [HD, KV, NCMP])
    rp = sb(att, "rp", [P, 4, HALVES * HEADS * ROPE_HALF])
    crp = sb(att, "crp", [NCMP, 4, KV * ROPE_HALF])
    gts = sb(att, "gts", [P, HALVES, 24])
    pr = sb(att, "pr", [P, 2, GQ, SEQ])
    pT = sb(att, "pT", [P, 2, 8, P])
    pc = sb(att, "pc", [P, HALVES, HEADS, NCMP])
    pcT = sb(att, "pcT", [NCMP, HEADS, P])
    nmx = sb(att, "nmx", [P, 8, GQ])
    den = sb(att, "den", [P, 8, GQ])
    cmx = sb(att, "cmx", [P, HALVES, HEADS])
    cden = sb(att, "cden", [P, HALVES, HEADS])
    otmp = sb(att, "otmp", [P, GQ * HD])
    SCALE = HD ** -0.5
    UNITS = [(t, br, g) for t in range(HALVES) for br in range(2) for g in range(KV)]
    VCOL = (NVS, NVW)

    with nc.Block(name="nsa", no_gpsimd_drain=True) as block:

        @block.sync
        def _(sp):
            for x, n in enumerate("kv"):
                load(sp, "small", w1[:, x, :, :], a["nsa_w1_" + n][0].rearrange("(l d) m -> d l m", d=HD))
                load(sp, "small", w2[:, x, :], a["nsa_w2_" + n][0])
                load(sp, "small", pe_[:, x, :], a["pe_" + n])

        @block.vector
        def _(dve):
            V = nc.vector

            def did(ins, *mark):
                ins.then_inc(dve_done, DV.one(mark or None))
                dve.wait_ge(dve_done, DV.n)

            def rope(x, n, cos, sin, tmp, *mark):
                x1, x2 = x[..., 0:ROPE_HALF], x[..., ROPE_HALF:2 * ROPE_HALF]
                t4 = [tmp[:, i, 0:n * ROPE_HALF].rearrange("p (n d) -> p n d", d=ROPE_HALF) for i in range(4)]
                for i, (s, c) in enumerate(((x1, cos), (x2, sin), (x2, cos), (x1, sin))):
                    did(V.tensor_tensor(t4[i], s, rep(c, n), ALU.mult))
                did(V.tensor_tensor(x1, t4[0], t4[1], ALU.subtract))
                did(V.tensor_tensor(x2, t4[2], t4[3], ALU.add), *mark)

            for t in range(HALVES):
                cs = [C(n)[:, t * ROPE_HALF:(t + 1) * ROPE_HALF] for n in ("cos", "sin")]
                for o, n, name in ((NQ, HEADS, "q"), (NKS, KV, "ks"), (NKW, KV, "kw")):
                    rope(nsa[:, t, o:o + n * HD].rearrange("p (n d) -> p n d", d=HD), n, *cs, rp, "rope", name, t)
            dve.wait_ge(*got("small"))
            for x, dst in enumerate((blk, blk2)):
                dve.wait_ge(*at("read", "cT", x, 1))
                for g in range(KV):
                    for half in range(2):
                        src = cT[:, x, g, 16 * half:16 * half + 16 * NCMP].rearrange("d (n b) -> d b n", b=16)
                        did(V.tensor_tensor(dst[:, 16 * half:16 * half + 16, g * NCMP:(g + 1) * NCMP], src,
                                            rep(pe_[:, x, 16 * half:16 * half + 16], NCMP, 2), ALU.add),
                            "blk", x, g, half)
            for x in range(2):
                dve.wait_ge(*at("hsg", x))
                did(V.tensor_tensor(hid[:, x, :], hid[:, x, :], hsg[:, x, :], ALU.mult), "hid", x)
            dve.wait_ge(*at("cmp"))
            did(V.tensor_copy(cmp_[:, :, :, :], bank_of("cmp")[0:NCMP, 0:4 * HD].rearrange(
                "p (x g d) -> p x g d", x=2, g=KV)), "read", "cmp")
            rope(cmp_[:, 0, :, :], KV, C("ccos", NCMP), C("csin", NCMP), crp, "crope")
            dve.wait_ge(*at("kcT"))
            did(V.tensor_copy(kcT[:, :, :], bank_of("kcT")[0:HD, 0:2 * NCMP].rearrange("p (g n) -> p g n", g=KV)),
                "read", "kcT")
            dve.wait_ge(*at("gates"))
            gv = gts[:, :, :].rearrange("p t (n b) -> p t n b", b=3)
            for t in range(HALVES):
                ok = C("cmpok")[:, t * NCMP:(t + 1) * NCMP]
                dve.wait_ge(*at("sc", t))
                did(V.tensor_scalar(pc[:, t], bank_of("sc", t)[:, 0:HEADS * NCMP].rearrange("p (n c) -> p n c", c=NCMP),
                                    SCALE, None, ALU.mult), "read", "sc", t)
                tm = rp[:, 0, 0:NCMP]
                did(V.tensor_scalar(tm, ok, 1.0, 1e30, ALU.subtract, ALU.mult))
                did(V.tensor_tensor(pc[:, t], pc[:, t], rep(tm, HEADS), ALU.add))
                did(V.tensor_reduce(cmx[:, t, :], pc[:, t], AX.X, ALU.max))
                did(V.tensor_tensor(pc[:, t], pc[:, t], rep(cmx[:, t, :], NCMP, 2), ALU.subtract), "cexp_in", t)
            for t in range(HALVES):
                ok = C("cmpok")[:, t * NCMP:(t + 1) * NCMP]
                dve.wait_ge(*at("cexp", t))
                did(V.tensor_reduce(cden[:, t, :], pc[:, t], AX.X, ALU.add))
                did(V.reciprocal(cden[:, t, :], cden[:, t, :]))
                did(V.tensor_tensor(pc[:, t], pc[:, t], rep(cden[:, t, :], NCMP, 2), ALU.mult))
                did(V.tensor_tensor(pc[:, t], pc[:, t], rep(ok, HEADS), ALU.mult), "pc", t)
                for q in range(2):
                    dve.wait_ge(*at("pcT", t, q))
                    if t:
                        dve.wait_ge(*at("oc", 0))
                    did(V.tensor_copy(pcT[:, 4 * q:4 * q + 4, :], bank_of("pcT", t, q)[0:NCMP, :].rearrange(
                        "p (n s) -> p n s", n=4)), "read", "pcT", t, q)
                dve.wait_ge(*at("oc", t))
                did(V.tensor_tensor(mix[:, t, RW:D].rearrange("p (n i) -> p n i", i=HD),
                                    bank_of("oc", t)[:, :].rearrange("p (n i) -> p n i", i=HD),
                                    rep(gv[:, t, :, 0], HD, 2), ALU.mult), "read", "oc", t)
            def scores(i):
                t, br, g = UNITS[i]
                p = pr[:, i % 2]
                if i >= 2:
                    dve.wait_ge(*at("ptT", i - 2, 0 if UNITS[i - 2][0] == 0 else 1))
                if t == 0:
                    dve.wait_ge(*at("s", i, 0))
                    did(V.scalar_tensor_tensor(out=p[:, :, 0:P], in0=bank_of("s", i, 0)[:, :].rearrange(
                        "p (n k) -> p n k", n=GQ), scalar=SCALE, in1=rep(C("causal")[:, P:2 * P], GQ), op0=ALU.mult,
                        op1=ALU.add), "read", "s", i, 0)
                else:
                    for j in range(2):
                        dve.wait_ge(*at("s", i, j))
                        did(V.scalar_tensor_tensor(out=p[:, 2 * j:2 * j + 2, :], in0=bank_of("s", i, j)[:, :].rearrange(
                            "p (n k) -> p n k", n=2), scalar=SCALE, in1=rep(C("causal"), 2), op0=ALU.mult,
                            op1=ALU.add), "read", "s", i, j)
                did(V.tensor_reduce(nmx[:, i, :], p[:, :, 0:P * (t + 1)], AX.X, ALU.max, negate=True), "nmx", i)

            def output(i):
                t, br, g = UNITS[i]
                dve.wait_ge(*at("exp", i))
                did(V.reciprocal(den[:, i, :], den[:, i, :]))
                did(V.tensor_tensor(den[:, i, :], den[:, i, :], gv[:, t, g * GQ:(g + 1) * GQ, br + 1], ALU.mult))
                dve.wait_ge(*at("o", i))
                o = mix[:, t, RW + g * GQ * HD:RW + (g + 1) * GQ * HD].rearrange("p (n i) -> p n i", i=HD)
                ot = otmp[:, :].rearrange("p (n i) -> p n i", i=HD)
                did(V.tensor_tensor(ot, bank_of("o", i)[:, 0:GQ * HD].rearrange("p (n i) -> p n i", i=HD),
                                    rep(den[:, i, :], HD, 2), ALU.mult), "read", "o", i)
                did(V.tensor_tensor(o, o, ot, ALU.add))

            scores(0)
            for i in range(len(UNITS)):
                if i + 1 < len(UNITS):
                    scores(i + 1)
                output(i)

        @block.scalar
        def _(act):
            S = nc.scalar
            S.activation(gts[:, :, :], nsa[:, :, NGATE:NGATE + 24], ACT.Sigmoid).then_inc(act_done, AC.one(("gates",)))
            for x in range(2):
                for g in range(KV):
                    act.wait_ge(*at("cT", x, g))
                    S.copy(cT[:, x, g, :], bank_of("cT", x, g)[0:HD, 0:SEQ]).then_inc(
                        act_done, AC.one(("read", "cT", x, g)))
            for j in range(4):
                act.wait_ge(*at("qT", j))
                S.copy(qT[:, 2 * j:2 * j + 2, :], bank_of("qT", j)[0:HD, :].rearrange("p (n t) -> p n t", n=2)).then_inc(
                    act_done, AC.one(("read", "qT", j)))
            for br in range(2):
                act.wait_ge(*at("kT", br))
                S.copy(kT[:, br, :, :], bank_of("kT", br)[0:HD, :].rearrange("p (n t) -> p n t", n=2)).then_inc(
                    act_done, AC.one(("read", "kT", br)))
            for x, n in enumerate("kv"):
                act.wait_ge(*at("hid", "mm", x))
                S.activation(hsg[:, x, :], bank_of("hid", "mm", x)[:, 0:2 * NCMP], ACT.Sigmoid,
                             bias=FT("b1_" + n)).then_inc(act_done, AC.one())
                S.activation(hid[:, x, :], bank_of("hid", "mm", x)[:, 0:2 * NCMP], ACT.Identity,
                             bias=FT("b1_" + n)).then_inc(act_done, AC.one(("hsg", x)))
                new[("read", "hid", "mm", x)] = ("act", AC.n)
            for t in range(HALVES):
                act.wait_ge(*at("cexp_in", t))
                S.activation(pc[:, t], pc[:, t], ACT.Exp).then_inc(act_done, AC.one(("cexp", t)))
            for i, (t, br, g) in enumerate(UNITS):
                act.wait_ge(*at("nmx", i))
                for n in range(GQ):
                    s = pr[:, i % 2, n, 0:P * (t + 1)]
                    S.activation(s, s, ACT.Exp, bias=nmx[:, i, n:n + 1], accum_out=den[:, i, n:n + 1]).then_inc(
                        act_done, AC.one())
                new[("exp", i)] = ("act", AC.n)
                for q in range(t + 1):
                    act.wait_ge(*at("ptT", i, q))
                    if i >= 2:
                        act.wait_ge(*at("o", i - 2))
                    S.copy(pT[:, i % 2, 4 * q:4 * q + 4, :], bank_of("ptT", i, q)[:, :].rearrange(
                        "p (n s) -> p n s", n=4)).then_inc(act_done, AC.one(("read", "ptT", i, q)))

        @block.tensor
        def _(pe):
            T = nc.tensor

            def heads_turned(job, src, cols, ready=()):
                for r in ready:
                    pe.wait_ge(*at(*r))
                b = take(pe, *job)
                for n, c in enumerate(cols):
                    for t in range(HALVES):
                        i = T.transpose(b[0:HD, n * SEQ + t * P:n * SEQ + (t + 1) * P], src[:, t, c:c + HD],
                                        C("ident"))
                i.then_inc(pe_done, PE.one(job))

            for x, o in enumerate((NKC, NVC)):
                for g in range(KV):
                    heads_turned(("cT", x, g), nsa, [o + g * HD])
            for j in range(4):
                heads_turned(("qT", j), nsa, [2 * j * HD, (2 * j + 1) * HD], [("rope", "q", 1)])
            for br, o in enumerate((NKS, NKW)):
                heads_turned(("kT", br), nsa, [o, o + HD], [("rope", "kw", 1)])
            for x, src in enumerate((blk, blk2)):
                pe.wait_ge(*at("blk", x, 1, 1))
                b = take(pe, "hid", "mm", x)
                for l in range(CBLK):
                    i = T.matmul(b[:, 0:2 * NCMP], w1[:, x, l, :], src[:, l, :], start=(l == 0), stop=(l == CBLK - 1))
                i.then_inc(pe_done, PE.one(("hid", "mm", x)))
            pe.wait_ge(*at("hid", 1))
            b = take(pe, "cmp")
            for x in range(2):
                for g in range(KV):
                    i = T.matmul(b[0:NCMP, (2 * x + g) * HD:(2 * x + g + 1) * HD],
                                 hid[:, x, g * NCMP:(g + 1) * NCMP], w2[:, x, :], start=True, stop=True)
            i.then_inc(pe_done, PE.one(("cmp",)))
            pe.wait_ge(*at("crope"))
            b = take(pe, "kcT")
            for g in range(KV):
                i = T.transpose(b[0:HD, g * NCMP:(g + 1) * NCMP], cmp_[:, 0, g, :], C("ident")[0:NCMP, 0:NCMP])
            i.then_inc(pe_done, PE.one(("kcT",)))
            pe.wait_ge(*at("read", "kcT"))
            pe.wait_ge(*at("read", "kT", 1))
            for t in range(HALVES):
                b = take(pe, "sc", t)
                for n in range(HEADS):
                    i = T.matmul(b[:, n * NCMP:(n + 1) * NCMP], qT[:, n, t * P:(t + 1) * P], kcT[:, n // GQ, :],
                                 start=True, stop=True)
                i.then_inc(pe_done, PE.one(("sc", t)))
            for t in range(HALVES):
                pe.wait_ge(*at("pc", t))
                for q in range(2):
                    b = take(pe, "pcT", t, q)
                    for n in range(4):
                        i = T.transpose(b[0:NCMP, n * P:(n + 1) * P], pc[:, t, 4 * q + n, :], C("ident"))
                    i.then_inc(pe_done, PE.one(("pcT", t, q)))
                b = take(pe, "oc", t)
                pe.wait_ge(*at("read", "pcT", t, 1))
                for n in range(HEADS):
                    i = T.matmul(b[:, n * HD:(n + 1) * HD], pcT[:, n, :], cmp_[:, 1, n // GQ, :], start=True,
                                 stop=True)
                i.then_inc(pe_done, PE.one(("oc", t)))

            def scores(i):
                t, br, g = UNITS[i]
                per = GQ // (t + 1)
                for j in range(t + 1):
                    b = take(pe, "s", i, j)
                    for n in range(per):
                        w = P * (t + 1)
                        m = T.matmul(b[:, n * w:(n + 1) * w], qT[:, g * GQ + j * per + n, t * P:(t + 1) * P],
                                     kT[:, br, g, 0:w], start=True, stop=True)
                    m.then_inc(pe_done, PE.one(("s", i, j)))

            scores(0)
            for i, (t, br, g) in enumerate(UNITS):
                if i + 1 < len(UNITS):
                    scores(i + 1)
                pe.wait_ge(*at("exp", i))
                for q in range(t + 1):
                    b = take(pe, "ptT", i, q)
                    for n in range(GQ):
                        m = T.transpose(b[:, n * P:(n + 1) * P], pr[:, i % 2, n, q * P:(q + 1) * P], C("ident"))
                    m.then_inc(pe_done, PE.one(("ptT", i, q)))
                pe.wait_ge(*at("read", "ptT", i, t))
                b = take(pe, "o", i)
                v0 = VCOL[br] + g * HD
                for n in range(GQ):
                    for q in range(t + 1):
                        m = T.matmul(b[:, n * HD:(n + 1) * HD], pT[:, i % 2, 4 * q + n, :], nsa[:, q, v0:v0 + HD],
                                     start=(q == 0), stop=(q == t))
                m.then_inc(pe_done, PE.one(("o", i)))
    att.close()

    def join(hy, tag, src, tiles, w_dram, mark_gate):
        srcT = sb(hy, "srcT_" + tag, [P, tiles, SEQ])
        wo = sb(hy, "wo_" + tag, [P, 4, 4, D])
        wv = w_dram.rearrange("(k p) n -> p k n", p=P)
        n0 = {n: loads[n] for n in loads}
        slots = ("w0", "w1", "w2", "par")

        with nc.Block(name="join_" + tag, no_gpsimd_drain=True) as block:

            @block.sync
            def _(sp):
                for q in range(tiles // 4):
                    load(sp, slots[q], wo[:, q, :, :], wv[:, 4 * q:4 * q + 4, :])

            @block.scalar
            def _(act):
                turn_act(act, tag, srcT, tiles)

            @block.vector
            def _(dve):
                for t in range(HALVES):
                    for c in range(2):
                        dve.wait_ge(*at("join", tag, t, c))
                        nc.vector.tensor_tensor(h[:, t, c * BANK:(c + 1) * BANK], bank_of("join", tag, t, c)[:, :],
                                                h[:, t, c * BANK:(c + 1) * BANK], ALU.add).then_inc(
                            dve_done, DV.one(("read", "join", tag, t, c)))

            @block.tensor
            def _(pe):
                turn_pe(pe, tag, src, tiles, mark_gate)
                bs = [[take(pe, "join", tag, t, c) for c in range(2)] for t in range(HALVES)]
                pe.wait_ge(*at("read", "turn", tag, 1, tiles // 4 - 1))
                for k in range(tiles):
                    if k % 4 == 0:
                        pe.wait_ge(s_ld[slots[k // 4]], n0[slots[k // 4]] + 16)
                    for t in range(HALVES):
                        for c in range(2):
                            i = nc.tensor.matmul(bs[t][c][:, :], srcT[:, k, t * P:(t + 1) * P],
                                                 wo[:, k // 4, k % 4, c * BANK:(c + 1) * BANK],
                                                 start=(k == 0), stop=(k == tiles - 1))
                            if k == tiles - 1:
                                i.then_inc(pe_done, PE.one(("join", tag, t, c)))

    with ExitStack() as hy:
        new[("mixed", 0)] = new[("mixed", 1)] = ("dve", DV.n)
        join(hy, "hyb", mix, 8, a["hyb_w_out"][0], ("mixed",))
    hyb.close()

    NRAW, NSPLIT = CHUNKS, CHUNKS
    PAIR = ((0, 1), (2, 3))
    ACC = (4, 5, 6, 7)
    EVENTS = ("hi", "lo", "used", "sel", "ga", "misc", "xa", "xb", "pt", "wcol", "gsb", "usb", "fold",
              "silu", "act", "ya", "yd", "sc", "shift")

    class Pass:

        def __init__(self, name):
            self.s = {k: sem(f"{name}_{k}") for k in EVENTS}
            self.raw = [sem(f"{name}_raw{c}") for c in range(NRAW)]
            self.seen = 0

    main_pass = Pass("m")
    over_pass = [Pass("o0"), Pass("o1")]

    def experts(layer):
        tag = f"ffn{layer}"
        moe = ExitStack()
        ux = sb(moe, "ux" + tag, [P, HALVES, KD, P])
        comb = sb(moe, "comb" + tag, [P, HALVES, EXPERTS])
        rank = sb(moe, "rank" + tag, [P, HALVES, EXPERTS])
        tiles_f = sb(moe, "tf" + tag, [P, 1])
        tiles_i = sb(moe, "ti" + tag, [P, 1], I32)

        raw = sb(moe, "raw" + tag, [P, NRAW, DC])
        srcs = [a["moe_w_gate"][layer].rearrange("e (p k) f -> e p (k f)", p=P),
                a["moe_w_up"][layer].rearrange("e (p k) f -> e p (k f)", p=P),
                a["moe_w_down"][layer].rearrange("e (p k) f -> e p (k f)", p=P)]

        def load_chunk(sp, ps, e, c):
            src = srcs[c // 2]
            sp.dma_start(raw[:, c, :], src[bass.ds(e, 1), :, (c % 2) * DC:(c % 2 + 1) * DC].rearrange(
                "e p n -> p (e n)")).then_inc(ps.raw[c], 16)

        rt_ = ExitStack()
        gain_ = sb(rt_, "gain" + tag, [P, D])
        junk_ = sb(rt_, "junk" + tag, [P, D])
        ss_, rstd_ = sb(rt_, "ss" + tag, [P, HALVES]), sb(rt_, "rstd" + tag, [P, HALVES])
        u_ = sb(rt_, "u" + tag, [P, HALVES, D])
        uT_ = sb(rt_, "uT" + tag, [P, KD, SEQ])
        rw_ = sb(rt_, "rw" + tag, [P, KD, EG + EXPERTS])
        rb_ = sb(rt_, "rb" + tag, [P, EG + EXPERTS])
        lg = sb(rt_, "lg" + tag, [P, HALVES, EG + EXPERTS])
        g8 = sb(rt_, "g8" + tag, [P, HALVES, 8])
        top = sb(rt_, "top" + tag, [P, HALVES, 8])
        topi = sb(rt_, "topi" + tag, [P, HALVES, 8], U32)
        idx = sb(rt_, "idx" + tag, [P, HALVES, 8])
        pen = sb(rt_, "pen" + tag, [P, HALVES, EG])
        le = sb(rt_, "le" + tag, [P, HALVES, EXPERTS])
        etop = sb(rt_, "etop" + tag, [P, HALVES, 8])
        etopi = sb(rt_, "etopi" + tag, [P, HALVES, 8], U32)
        eidx = sb(rt_, "eidx" + tag, [P, HALVES, 8])
        gsum = sb(rt_, "gsum" + tag, [P, HALVES])
        ngm = sb(rt_, "ngm" + tag, [P, HALVES])
        de = sb(rt_, "de" + tag, [P, HALVES])
        w01 = sb(rt_, "w01" + tag, [P, HALVES, 2])
        hit = sb(rt_, "hit" + tag, [P, HALVES, EXPERTS])
        hit2 = sb(rt_, "hit2" + tag, [P, HALVES, EXPERTS])
        cnt = sb(rt_, "cnt" + tag, [P, 4])
        n0 = dict(loads)
        new[("h", tag, 0)] = new[("h", tag, 1)] = ("dve", DV.n)

        with nc.Block(name="router" + tag, no_gpsimd_drain=True) as block:

            @block.sync
            def _(sp):
                load(sp, "gain", gain_[:, :], row_src(tag))
                load(sp, "small", rw_[:, :, :], a["router"][layer].rearrange("(k p) n -> p k n", p=P))
                load(sp, "small", rb_[:, :], row_src(f"rb{layer}"))
                for c in range(CHUNKS):
                    load_chunk(sp, main_pass, 0, c)

            @block.vector
            def _(dve):
                V = nc.vector

                def did(ins, *mark):
                    ins.then_inc(dve_done, DV.one(mark or None))
                    dve.wait_ge(dve_done, DV.n)

                did(V.memset(g8[:, :, :], NEG))
                norm_dve(dve, tag, rstd_, u_, gain_, s_ld["gain"], n0["gain"] + 16)
                ids = C("slots")[:, 0:EXPERTS]
                dve.wait_ge(s_ld["small"], n0["small"] + 32)
                for t in range(HALVES):
                    dve.wait_ge(*at("logits", tag, t))
                    did(V.tensor_tensor(lg[:, t, :], bank_of("logits", tag, t)[:, 0:EG + EXPERTS], rb_[:, :],
                                        ALU.add), "read", "logits", tag, t)
                    did(V.tensor_copy(g8[:, t, 0:EG], lg[:, t, 0:EG]))
                    did(V.max(out=top[:, t, :], in_=g8[:, t, :]))
                    did(V.max_index(out=topi[:, t, :], in_max=top[:, t, :], in_values=g8[:, t, :]))
                    did(V.tensor_copy(idx[:, t, :], topi[:, t, :]))
                    did(V.tensor_scalar(ngm[:, t:t + 1], top[:, t, 0:1], -1.0, None, ALU.mult), "ngm", tag, t)
                    did(V.tensor_scalar(pen[:, t, :], ids[:, 0:EG], idx[:, t, 0:1], None, ALU.is_equal))
                    did(V.tensor_scalar(pen[:, t, :], pen[:, t, :], 1.0, 1e30, ALU.subtract, ALU.mult))
                    did(V.tensor_tensor(le[:, t, :].rearrange("p (g e) -> p g e", g=EG),
                                        lg[:, t, EG:].rearrange("p (g e) -> p g e", g=EG),
                                        rep(pen[:, t, :], EPG, 2), ALU.add))
                    did(V.max(out=etop[:, t, :], in_=le[:, t, :]))
                    did(V.max_index(out=etopi[:, t, :], in_max=etop[:, t, :], in_values=le[:, t, :]))
                    did(V.tensor_copy(eidx[:, t, :], etopi[:, t, :]))
                    did(V.tensor_tensor(de[:, t:t + 1], etop[:, t, 1:2], etop[:, t, 0:1], ALU.subtract),
                        "de", tag, t)
                for t in range(HALVES):
                    dve.wait_ge(*at("rexp", tag, t))
                    did(V.tensor_scalar(w01[:, t, 0:1], de[:, t:t + 1], 1.0, gsum[:, t:t + 1], ALU.add, ALU.mult))
                    did(V.reciprocal(w01[:, t, 0:1], w01[:, t, 0:1]))
                    did(V.tensor_tensor(w01[:, t, 1:2], w01[:, t, 0:1], de[:, t:t + 1], ALU.mult))
                    for dst, one in ((comb, False), (hit, True)):
                        for j, o in enumerate((dst, hit2)):
                            s2 = 1.0 if one else w01[:, t, j:j + 1]
                            did(V.tensor_scalar(o[:, t, :], ids, eidx[:, t, j:j + 1], s2, ALU.is_equal, ALU.mult))
                        did(V.tensor_tensor(dst[:, t, :], dst[:, t, :], hit2[:, t, :], ALU.add), "hit" if one
                            else "comb", tag, t)
                dve.wait_ge(*at("rank", tag))
                rb = bank_of("rank", tag)
                for t in range(HALVES):
                    did(V.scalar_tensor_tensor(out=rank[:, t, :], in0=hit[:, t, :], scalar=-1000.0,
                                               in1=rb[:, t * EXPERTS:(t + 1) * EXPERTS], op0=ALU.mult, op1=ALU.add))
                did(V.tensor_scalar(rank[:, :, :], rank[:, :, :], 1000.0, None, ALU.add))
                did(V.tensor_reduce(cnt[:, 0:1], rb[:, 2 * EXPERTS:3 * EXPERTS], AX.X, ALU.max), "read", "rank", tag)
                for j in range(1, 4):
                    did(V.tensor_scalar(cnt[:, j:j + 1], cnt[:, 0:1], float(CAP * j), None, ALU.is_gt))
                did(V.tensor_reduce(tiles_f[:, :], cnt[:, 1:4], AX.X, ALU.add))
                did(V.tensor_scalar(tiles_f[:, :], tiles_f[:, :], 1.0, None, ALU.add))
                did(V.tensor_copy(tiles_i[:, :], tiles_f[:, :]))

            @block.scalar
            def _(act):
                S = nc.scalar
                norm_act(act, tag, junk_, ss_, rstd_)
                turn_act(act, tag, uT_, KD)
                for t in range(HALVES):
                    S.copy(ux[:, t], u_[:, t, :].rearrange("p (q k) -> p k q", k=KD)).then_inc(
                        act_done, AC.one(("uhi", tag, t)))
                for t in range(HALVES):
                    act.wait_ge(*at("de", tag, t))
                    S.activation(g8[:, t, 0:EG], g8[:, t, 0:EG], ACT.Exp, bias=ngm[:, t:t + 1],
                                 accum_out=gsum[:, t:t + 1]).then_inc(act_done, AC.one())
                    S.activation(de[:, t:t + 1], de[:, t:t + 1], ACT.Exp).then_inc(act_done,
                                                                                 AC.one(("rexp", tag, t)))

            @block.tensor
            def _(pe):
                turn_pe(pe, tag, u_, KD, ("u", tag))
                pe.wait_ge(*at("read", "turn", tag, 1, 1))
                pe.wait_ge(s_ld["small"], n0["small"] + 32)
                for t in range(HALVES):
                    b = take(pe, "logits", tag, t)
                    for k in range(KD):
                        i = nc.tensor.matmul(b[:, 0:EG + EXPERTS], uT_[:, k, t * P:(t + 1) * P], rw_[:, k, :],
                                             start=(k == 0), stop=(k == KD - 1))
                    i.then_inc(pe_done, PE.one(("logits", tag, t)))
                pe.wait_ge(*at("hit", tag, 1))
                b = take(pe, "rank", tag)
                r0, r1, r2 = (b[:, i * EXPERTS:(i + 1) * EXPERTS] for i in range(3))
                nc.tensor.matmul(r0, C("before"), hit[:, 0, :], start=True, stop=True)
                nc.tensor.matmul(r1, C("ones"), hit[:, 0, :], start=True, stop=False)
                nc.tensor.matmul(r1, C("before"), hit[:, 1, :], start=False, stop=True)
                nc.tensor.matmul(r2, C("ones"), hit[:, 0, :], start=True, stop=False)
                nc.tensor.matmul(r2, C("ones"), hit[:, 1, :], start=False, stop=True).then_inc(
                    pe_done, PE.one(("rank", tag)))
        rt_.close()

        whi = sb(moe, "whi" + tag, [P, NSPLIT, DC], F32R)
        wlo = sb(moe, "wlo" + tag, [P, NSPLIT, DC], F32R)
        sel = sb(moe, "sel" + tag, [P, HALVES, 2, P])
        ccol = sb(moe, "ccol" + tag, [P, HALVES, 2])
        xg = sb(moe, "xg" + tag, [P, 2, KD, P], F32R)
        selT = sb(moe, "selT" + tag, [P, 2, SEQ], F32R)
        wcol = sb(moe, "wcol" + tag, [P, 2])
        gu = sb(moe, "gu" + tag, [P, 2, 4, P])
        sg = sb(moe, "sg" + tag, [P, 4, CAP])
        af = sb(moe, "af" + tag, [P, 4, CAP])
        aT = sb(moe, "aT" + tag, [P, 4, P], F32R)
        ys = sb(moe, "ys" + tag, [P, 2, D], F32R)

        def slot_free(eng, S, b0, e, c):
            if not isinstance(e, int) or CHUNKS * e + c >= NSPLIT:
                eng.wait_ge(S["used"], CHUNKS * (b0 + e) + c - NSPLIT + 1)

        def every_expert(eng, run):
            run(0, 0, True, 0)
            run(1, 1, False, 0)
            with eng.Fori(1, EXPERTS // 2 - 1) as i:
                run(i * 2, 0, False, 0)
                run(i * 2 + 1, 1, False, 0)
            run(EXPERTS - 2, 0, False, 1)
            run(EXPERTS - 1, 1, False, 2)

        def sync_pass(sp, ps, b0, loaded):
            S = ps.s

            def run(e, odd, first, last):
                for c in range(CHUNKS):
                    if not first:
                        sp.wait_ge(S["lo"], CHUNKS * (b0 + e - 1) + c + 1)
                    if not (first and loaded):
                        load_chunk(sp, ps, e, c)

            every_expert(sp, run)

        def act_pass(act, ps, b0):
            S = ps.s

            def hi(e, e2, c):
                act.wait_ge(ps.raw[c], 16 * (b0 + e + 1))
                slot_free(act, S, b0, e, c)
                nc.scalar.copy(whi[:, c, :], raw[:, c, :]).then_inc(S["hi"], 1)

            def evict_x(e, o):
                act.wait_ge(S["ga"], b0 + e + 2)
                for n in range(2):
                    nc.scalar.copy(xg[:, :, 4 * n:4 * n + 4, 0:CAP].rearrange("p x k s -> p k x s"),
                                   bank[PAIR[o][n]][:, :].rearrange("p (k x s) -> p k x s", k=4, x=2)).then_inc(
                        S["xa"], 1)

            def evict_selT(e, e2, o):
                act.wait_ge(S["wcol"], b0 + e + 1)
                nc.scalar.copy(selT[:, e2, :], bank[PAIR[o][1]][:, 0:SEQ]).then_inc(S["pt"], 1)

            def evict_y(e, e2):
                act.wait_ge(S["used"], CHUNKS * (b0 + e + 1))
                act.wait_ge(S["wcol"], b0 + e + 1)
                for n in range(2):
                    nc.scalar.activation(ys[:, 0, n * BANK:(n + 1) * BANK], bank[PAIR[e2][n]][:, :], ACT.Copy,
                                         scale=wcol[:, e2:e2 + 1]).then_inc(S["ya"], 1)

            def evict_gu(e, odd, x):
                act.wait_ge(S["used"], CHUNKS * (b0 + e) + 2 + 2 * x)
                nc.scalar.copy(gu[:, x], bank[PAIR[odd][x]][:, :].rearrange("p (q j) -> p j q", j=4)).then_inc(
                    S["usb" if x else "gsb"], 1)

            hi(0, 0, 0)
            hi(0, 0, 1)
            evict_x(0, 0)
            evict_selT(0, 0, 0)

            def run(e, odd, first, last):
                o = 1 - odd
                hi(e, odd, 2)
                if not first:
                    evict_y(e - 1, o)
                if not odd and not first:
                    act.wait_ge(S["sc"], b0 + e - 1)
                    evict_selT(e, 0, 0)
                hi(e, odd, 3)
                hi(e, odd, 4)
                evict_gu(e, odd, 0)
                hi(e, odd, 5)
                evict_gu(e, odd, 1)
                if last < 2:
                    hi(e + 1, o, 0)
                act.wait_ge(S["fold"], b0 + e + 1)
                nc.scalar.activation(sg[:, :, :], bank[PAIR[odd][0]][:, :].rearrange(
                    "p (j x s) -> p j x s", j=4, x=2)[:, :, 0, :], ACT.Silu).then_inc(S["silu"], 1)
                if odd and last < 2:
                    evict_x(e + 1, o)
                if last < 2:
                    hi(e + 1, o, 1)
                if not odd:
                    if not first:
                        act.wait_ge(S["sc"], b0 + e)
                    evict_selT(e + 1, 1, 1)

            every_expert(act, run)
            evict_y(EXPERTS - 1, 1)

        def dve_pass(dve, ps, b0):
            S = ps.s
            V = nc.vector

            def lo(e, e2, c):
                dve.wait_ge(S["hi"], CHUNKS * (b0 + e) + c + 1)
                slot_free(dve, S, b0, e, c)
                V.tensor_tensor(wlo[:, c, :], raw[:, c, :], whi[:, c, :].bitcast(F32), ALU.subtract).then_inc(
                    S["lo"], 1)

            def select(e):
                if not (isinstance(e, int) and e == 0):
                    dve.wait_ge(S["misc"], b0 + e)
                for t in range(HALVES):
                    for x in range(2):
                        V.tensor_scalar(sel[:, t, x, :], C("slots"), rank[:, t, bass.ds(e + x, 1)], None,
                                        ALU.is_equal)
                V.tensor_copy(ccol[:, :, :], comb[:, :, bass.ds(e, 2)]).then_inc(S["sel"], 2)

            def weights(e, e2, o):
                dve.wait_ge(S["misc"], b0 + e + 1)
                V.tensor_copy(wcol[:, e2:e2 + 1], bank[PAIR[o][1]][:, SEQ:SEQ + 1]).then_inc(S["wcol"], 1)

            def low_x(e, o):
                for n in range(2):
                    dve.wait_ge(S["xa"], b0 + e + n + 1)
                    V.tensor_tensor(xg[:, :, 4 * n:4 * n + 4, CAP:P].rearrange("p x k s -> p k x s"),
                                    bank[PAIR[o][n]][:, :].rearrange("p (k x s) -> p k x s", k=4, x=2),
                                    xg[:, :, 4 * n:4 * n + 4, 0:CAP].rearrange("p x k s -> p k x s").bitcast(F32),
                                    ALU.subtract).then_inc(S["xb"], 1)

            def evict_y(e, e2):
                dve.wait_ge(S["wcol"], b0 + e + 1)
                for n in range(2):
                    dve.wait_ge(S["ya"], 2 * (b0 + e) + n + 1)
                    V.scalar_tensor_tensor(out=ys[:, 1, n * BANK:(n + 1) * BANK], in0=bank[PAIR[e2][n]][:, :],
                                           scalar=wcol[:, e2:e2 + 1],
                                           in1=ys[:, 0, n * BANK:(n + 1) * BANK].bitcast(F32), op0=ALU.mult,
                                           op1=ALU.subtract).then_inc(S["yd"], 1)

            def activate(e, o):
                dve.wait_ge(S["silu"], b0 + e + 1)
                V.tensor_tensor(af[:, :, :], bank[PAIR[1 - o][0]][:, :].rearrange(
                    "p (j x s) -> p j x s", j=4, x=2)[:, :, 1, :], sg[:, :, :], ALU.mult).then_inc(S["act"], 1)
                dve.wait_ge(S["act"], 3 * (b0 + e) + 1)
                V.tensor_copy(aT[:, :, 0:CAP], af[:, :, :]).then_inc(S["act"], 1)
                dve.wait_ge(S["act"], 3 * (b0 + e) + 2)
                V.tensor_tensor(aT[:, :, CAP:P], af[:, :, :], aT[:, :, 0:CAP].bitcast(F32),
                                ALU.subtract).then_inc(S["act"], 1)

            select(0)
            lo(0, 0, 0)
            low_x(0, 0)
            weights(0, 0, 0)
            lo(0, 0, 1)

            def run(e, odd, first, last):
                o = 1 - odd
                if not first:
                    evict_y(e - 1, o)
                if not odd and not first:
                    weights(e, 0, 0)
                lo(e, odd, 2)
                lo(e, odd, 3)
                if not odd:
                    weights(e + 1, o, o)
                    if not last:
                        select(e + 2)
                lo(e, odd, 4)
                lo(e, odd, 5)
                activate(e, o)
                if odd and last < 2:
                    low_x(e + 1, o)
                if last < 2:
                    lo(e + 1, o, 0)
                    lo(e + 1, o, 1)

            every_expert(dve, run)
            evict_y(EXPERTS - 1, 1)

        def pe_pass(pe, ps, b0, opens):
            S = ps.s
            T = nc.tensor

            def gather(e, o):
                pe.wait_ge(S["sel"], b0 + e + 2)
                for k in range(KD):
                    b = bank[PAIR[o][k // 4]]
                    for t in range(HALVES):
                        i = T.matmul(b[:, (k % 4) * P:(k % 4 + 1) * P].rearrange("p (x s) -> p x s", x=2),
                                     ux[:, t, k, :], sel[:, t, :, 0:CAP], start=(t == 0), stop=(t == HALVES - 1))
                i.then_inc(S["ga"], 2)

            def misc(e, e2, o):
                b = bank[PAIR[o][1]]
                for t in range(HALVES):
                    T.transpose(b[:, t * P:(t + 1) * P], sel[:, t, e2, :], C("ident"))
                for t in range(HALVES):
                    i = T.matmul(b[:, SEQ:SEQ + 1], sel[:, t, e2, :], ccol[:, t, e2:e2 + 1], start=(t == 0),
                                 stop=(t == HALVES - 1))
                i.then_inc(S["misc"], 1)

            def project(e, e2, c):
                pe.wait_ge(S["lo"], CHUNKS * (b0 + e) + c + 1)
                b = bank[PAIR[e2][c // 2]]
                for k in range(4):
                    for w in (whi, wlo):
                        i = T.matmul(b[:, :], xg[:, e2, 4 * (c % 2) + k, :], w[:, c, k * FH:(k + 1) * FH],
                                     start=(c % 2 == 0 and k == 0 and w is whi),
                                     stop=(c % 2 == 1 and k == 3 and w is wlo))
                i.then_inc(S["used"], 1)

            def scatter(e, e2, part, start):
                t, n = part // 2, part % 2
                for x in range(2):
                    i = T.matmul(bank[ACC[part]][:, :], selT[:, e2, t * P:(t + 1) * P],
                                 ys[:, x, n * BANK:(n + 1) * BANK], start=start and x == 0, stop=False)
                if part == 3:
                    i.then_inc(S["sc"], 1)

            gather(0, 0)
            pe.wait_ge(S["xb"], b0 + 2)
            misc(0, 0, 0)

            def run(e, odd, first, last):
                o = 1 - odd
                opening = opens and isinstance(e, int) and e == 1
                pe.wait_ge(S["xb"], b0 + e + 2 - odd)
                project(e, odd, 0)
                project(e, odd, 1)
                pe.wait_ge(S["pt"], b0 + e + 1)
                project(e, odd, 2)
                if not first:
                    pe.wait_ge(S["yd"], 2 * (b0 + e))
                if not odd:
                    misc(e + 1, o, o)
                project(e, odd, 3)
                if not first:
                    scatter(e - 1, o, 0, opening)
                pe.wait_ge(S["gsb"], b0 + e + 1)
                pe.wait_ge(S["usb"], b0 + e + 1)
                b = bank[PAIR[odd][0]]
                for j in range(4):
                    for x in range(2):
                        i = T.matmul(b[:, (2 * j + x) * CAP:(2 * j + x + 1) * CAP], gu[:, x, j, :], C("fold"),
                                     start=True, stop=True)
                i.then_inc(S["fold"], 1)
                if odd and last < 2:
                    gather(e + 1, o)
                if not first:
                    for part in (1, 2, 3):
                        scatter(e - 1, o, part, opening)
                pe.wait_ge(S["act"], 3 * (b0 + e + 1))
                for c in (4, 5):
                    pe.wait_ge(S["lo"], CHUNKS * (b0 + e) + c + 1)
                    for jj in range(2):
                        j = 2 * (c - 4) + jj
                        for n in range(2):
                            for w in (whi, wlo):
                                i = T.matmul(bank[PAIR[odd][n]][:, :], aT[:, j, :],
                                             w[:, c, jj * D + n * BANK:jj * D + (n + 1) * BANK],
                                             start=(j == 0 and w is whi), stop=(j == 3 and w is wlo))
                    i.then_inc(S["used"], 1)
                if odd and last < 2:
                    pe.wait_ge(S["xb"], b0 + e + 3)
                    misc(e + 1, o, o)

            every_expert(pe, run)
            pe.wait_ge(S["yd"], 2 * (b0 + EXPERTS))
            for part in range(4):
                scatter(EXPERTS - 1, 1, part, False)

        base = main_pass.seen
        with nc.Block(name="experts" + tag, no_gpsimd_drain=True) as block:

            @block.sync
            def _(sp):
                sync_pass(sp, main_pass, base, True)

            @block.scalar
            def _(act):
                act_pass(act, main_pass, base)

            @block.vector
            def _(dve):
                dve_pass(dve, main_pass, base)

            @block.tensor
            def _(pe):
                pe_pass(pe, main_pass, base, True)
        main_pass.seen += EXPERTS

        ov = over_pass[layer]

        def more(eng, body):
            n = eng.value_load(tiles_i[0:1, 0:1], min_val=1, max_val=4)
            with eng.If(n > 1):
                with eng.Fori(1, n) as tau:
                    body(tau)

        with nc.Block(name="overflow" + tag, no_gpsimd_drain=True) as block:

            @block.sync
            def _(sp):
                def body(tau):
                    sp.wait_ge(ov.s["shift"], tau)
                    sync_pass(sp, ov, (tau - 1) * EXPERTS, False)

                more(sp, body)

            @block.scalar
            def _(act):
                def body(tau):
                    act.wait_ge(ov.s["shift"], tau)
                    act_pass(act, ov, (tau - 1) * EXPERTS)

                more(act, body)

            @block.vector
            def _(dve):
                def body(tau):
                    nc.vector.tensor_scalar(rank[:, :, :], rank[:, :, :], float(CAP), None, ALU.subtract).then_inc(
                        ov.s["shift"], 1)
                    dve.wait_ge(ov.s["shift"], tau)
                    dve_pass(dve, ov, (tau - 1) * EXPERTS)
                    dve.wait_ge(ov.s["sc"], tau * EXPERTS)

                more(dve, body)

            @block.tensor
            def _(pe):
                def body(tau):
                    pe.wait_ge(ov.s["shift"], tau)
                    pe_pass(pe, ov, (tau - 1) * EXPERTS, False)

                more(pe, body)


        with nc.Block(name="close" + tag, no_gpsimd_drain=True) as block:

            @block.tensor
            def _(pe):
                for t in range(HALVES):
                    for n in range(2):
                        nc.tensor.matmul(bank[ACC[2 * t + n]][:, :], C("ident"), h[:, t, n * BANK:(n + 1) * BANK],
                                         start=False, stop=True).then_inc(pe_done, PE.one(("close", tag, t, n)))

            @block.vector
            def _(dve):
                for t in range(HALVES):
                    for n in range(2):
                        dve.wait_ge(*at("close", tag, t, n))
                        nc.vector.tensor_copy(h[:, t, n * BANK:(n + 1) * BANK], bank[ACC[2 * t + n]][:, :]).then_inc(
                            dve_done, DV.one())
        moe.close()
        turn["last"] = [None] * 8

    experts(0)

    new[("h", "mix1", 0)] = new[("h", "mix1", 1)] = ("dve", DV.n)
    mam = ExitStack()
    zs = sb(mam, "zs", [P, HALVES, DI])
    xc = sb(mam, "xc", [P, NXT, SEQ])
    dtv = sb(mam, "dtv", [P, HALVES, MH])
    mpar = sb(mam, "mpar", [P, 3 * MH + DI])
    mp = ExitStack()
    gain2 = sb(mp, "gain2", [P, D])
    ss2, rstd2 = sb(mp, "ss2", [P, HALVES]), sb(mp, "rstd2", [P, HALVES])
    u2 = sb(mp, "u2", [P, HALVES, D])
    uT2 = sb(mp, "uT2", [P, KD, SEQ])
    wr2 = sb(mp, "wr2", [P, 3, KD, BANK])
    xr = sb(mp, "xr", [P, NXT, SEQ + 3])
    junk2 = xc[:, 0:4, :].rearrange("p c t -> p (c t)")
    MG = [(DI + BANK * g, BANK, "x") for g in range(6)] + [(DI + XBC, MH, "dt")] + \
         [(BANK * g, BANK, "z") for g in range(4)]
    w_ssm = a["ssm_w_in"][0].rearrange("(k p) n -> p k n", p=P)
    ring0 = {n: loads[n] for n in loads}

    with nc.Block(name="ssm_in", no_gpsimd_drain=True) as block:

        @block.sync
        def _(sp):
            load(sp, "gain", gain2[:, :], row_src("mix1"))
            for g, (c0, n, _) in enumerate(MG):
                if g >= 3:
                    sp.wait_ge(*at("mgroup", g - 3))
                load(sp, f"w{g % 3}", wr2[:, g % 3, :, 0:n], w_ssm[:, :, c0:c0 + n])
            for i, name in enumerate(("dt_bias", "a_log", "d")):
                load(sp, "small", mpar[:, i * MH:(i + 1) * MH], row_src(name))
            load(sp, "small", mpar[:, 3 * MH:], row_src("ssm_norm"))

        @block.vector
        def _(dve):
            V = nc.vector
            V.memset(xr[:, :, 0:3], 0.0).then_inc(dve_done, DV.one(("xr0",)))
            norm_dve(dve, "mix1", rstd2, u2, gain2, s_ld["gain"], ring0["gain"] + 16)
            dve.wait_ge(dve_done, DV.n)
            for j in range(NXT):
                dve.wait_ge(*at("read", "xbc", j // 2))
                w = lambda k: FT("conv_w")[:, k * NXT + j:k * NXT + j + 1]
                V.tensor_scalar(xc[:, j, :], xr[:, j, 0:SEQ], w(0), None, ALU.mult).then_inc(dve_done, DV.one())
                for k in range(1, 4):
                    dve.wait_ge(dve_done, DV.n)
                    V.scalar_tensor_tensor(out=xc[:, j, :], in0=xr[:, j, k:k + SEQ], scalar=w(k), in1=xc[:, j, :],
                                           op0=ALU.mult, op1=ALU.add).then_inc(
                        dve_done, DV.one(("conv", j) if k == 3 else None))
            for t in range(HALVES):
                dve.wait_ge(*at("dt", t))
                V.tensor_copy(dtv[:, t, :], bank_of("dt", t)[:, 0:MH]).then_inc(dve_done, DV.one(("read", "dt", t)))

        @block.scalar
        def _(act):
            S = nc.scalar
            norm_act(act, "mix1", junk2, ss2, rstd2)
            turn_act(act, "mix1", uT2, KD)

            def conv_silu(j):
                act.wait_ge(*at("conv", j))
                S.activation(xc[:, j, :], xc[:, j, :], ACT.Silu, bias=FT("conv_b")[:, j:j + 1]).then_inc(
                    act_done, AC.one(("xc", j)))

            act.wait_ge(*at("xr0"))
            for j in range(NXT // 2):
                act.wait_ge(*at("xbc", j))
                S.copy(xr[:, 2 * j:2 * j + 2, 3:SEQ + 3], bank_of("xbc", j)[:, :].rearrange(
                    "p (c t) -> p c t", c=2)).then_inc(act_done, AC.one(("read", "xbc", j)))
            for g in range(4):
                for t in range(HALVES):
                    act.wait_ge(*at("z", g, t))
                    S.activation(zs[:, t, g * BANK:(g + 1) * BANK], bank_of("z", g, t)[:, :], ACT.Silu).then_inc(
                        act_done, AC.one(("read", "z", g, t)))
                for j in range(6 * g, 6 * g + 6):
                    conv_silu(j)

        @block.tensor
        def _(pe):
            turn_pe(pe, "mix1", u2, KD, ("u", "mix1"))
            pe.wait_ge(*at("read", "turn", "mix1", 1, 1))
            for g, (c0, n, kind) in enumerate(MG):
                pe.wait_ge(s_ld[f"w{g % 3}"], ring0[f"w{g % 3}"] + 16 * (g // 3 + 1))
                for j in range(2):
                    if kind == "x":
                        b = take(pe, "xbc", 2 * g + j)
                        for c in range(2):
                            for k in range(KD):
                                i = nc.tensor.matmul(b[:, c * SEQ:(c + 1) * SEQ],
                                                     wr2[:, g % 3, k, (2 * j + c) * P:(2 * j + c + 1) * P],
                                                     uT2[:, k, :], start=(k == 0), stop=(k == KD - 1))
                        i.then_inc(pe_done, PE.one(("xbc", 2 * g + j)))
                    else:
                        job = ("dt", j) if kind == "dt" else ("z", g - 7, j)
                        b = take(pe, *job)
                        for k in range(KD):
                            i = nc.tensor.matmul(b[:, 0:n], uT2[:, k, j * P:(j + 1) * P], wr2[:, g % 3, k, 0:n],
                                                 start=(k == 0), stop=(k == KD - 1))
                        i.then_inc(pe_done, PE.one(job))
                new[("mgroup", g)] = ("pe", PE.n)
    mp.close()

    ssd = ExitStack()
    xt = sb(ssd, "xt", [P, HALVES, DI])
    xdt = sb(ssd, "xdt", [P, HALVES, DI])
    BW = 3 * P
    cb = sb(ssd, "cb", [P, GROUPS, BW])
    ring = sb(ssd, "ring", [P, 3, 2, BW])
    acs = sb(ssd, "acs", [P, HALVES, MH])
    ad = sb(ssd, "ad", [P, HALVES, MH])
    tmp2 = sb(ssd, "tmp2", [P, 2, HALVES * MH])
    csT = sb(ssd, "csT", [MH, SEQ])
    sq2 = sb(ssd, "sq2", [P, BANK])
    rs = sb(ssd, "rs", [P, HALVES * GROUPS])
    HPG = MH // GROUPS

    with nc.Block(name="ssd", no_gpsimd_drain=True) as block:

        @block.gpsimd
        def _(pool):
            G = nc.gpsimd
            for t in range(HALVES):
                for g in range(GROUPS):
                    pool.wait_ge(*at("read", "xt", t, g))
                    pool.wait_ge(*at("dtok"))
                    o = slice(g * BANK, (g + 1) * BANK)
                    G.tensor_tensor(xdt[:, t, o].rearrange("p (n i) -> p n i", i=HD),
                                    xt[:, t, o].rearrange("p (n i) -> p n i", i=HD),
                                    rep(dtv[:, t, g * HPG:(g + 1) * HPG], HD, 2), ALU.mult).then_inc(
                        pool_done, PO.one(("xdt", t, g)))

        @block.vector
        def _(dve):
            V = nc.vector

            def did(ins, *mark):
                ins.then_inc(dve_done, DV.one(mark or None))
                dve.wait_ge(dve_done, DV.n)

            dve.wait_ge(*got("small"))
            did(V.tensor_tensor(dtv[:, :, :], dtv[:, :, :], rep(mpar[:, 0:MH], HALVES), ALU.add))
            did(V.tensor_scalar(ad[:, :, :], dtv[:, :, :], 0.0, None, ALU.max))
            did(V.scalar_tensor_tensor(out=dtv[:, :, :], in0=ad[:, :, :], scalar=-2.0, in1=dtv[:, :, :],
                                       op0=ALU.mult, op1=ALU.add), "nabs")
            dve.wait_ge(*at("ln1p"))
            did(V.tensor_tensor(dtv[:, :, :], dtv[:, :, :], ad[:, :, :], ALU.add), "dtok")
            did(V.scalar_tensor_tensor(out=ad[:, :, :], in0=dtv[:, :, :], scalar=-1.0,
                                       in1=rep(mpar[:, MH:2 * MH], HALVES), op0=ALU.mult, op1=ALU.mult), "ad")
            dve.wait_ge(*at("acs"))
            did(V.tensor_copy(acs[:, :, :], bank_of("acs")[:, 0:HALVES * MH].rearrange("p (t n) -> p t n", t=2)),
                "read", "acs")
            dve.wait_ge(*at("csT"))
            did(V.tensor_copy(csT[:, :], bank_of("csT")[0:MH, 0:SEQ]), "read", "csT")
            for g in range(GROUPS):
                dve.wait_ge(*at("cb", g))
                b = bank_of("cb", g)
                did(V.tensor_tensor(cb[:, g, 0:P], b[:, 0:P], C("upto"), ALU.mult))
                did(V.tensor_copy(cb[:, g, P:2 * P], b[:, P:2 * P]))
                did(V.tensor_tensor(cb[:, g, 2 * P:3 * P], b[:, 2 * P:3 * P], C("upto"), ALU.mult), "read", "cb", g)

            def decays(i):
                dve.wait_ge(*at("row", i))
                if i >= 3:
                    dve.wait_ge(*at("used", i - 3))
                for e in range(2):
                    n = 2 * i + e
                    b = bank_of("row", i)[:, e * SEQ:(e + 1) * SEQ]
                    V.tensor_scalar(ring[:, i % 3, e, 0:SEQ], b, acs[:, 0, n:n + 1], 0.0, ALU.subtract,
                                    ALU.min).then_inc(dve_done, DV.one())
                    V.tensor_scalar(ring[:, i % 3, e, SEQ:BW], b[:, P:SEQ], acs[:, 1, n:n + 1], 0.0, ALU.subtract,
                                    ALU.min).then_inc(dve_done, DV.one())
                new[("read", "row", i)] = new[("dec", i)] = ("dve", DV.n)

            def finish(g):
                o = slice(g * BANK, (g + 1) * BANK)
                for t in range(HALVES):
                    dve.wait_ge(*at("xdt", t, g))
                    did(V.tensor_tensor(xt[:, t, o].rearrange("p (n i) -> p n i", i=HD),
                                        xt[:, t, o].rearrange("p (n i) -> p n i", i=HD),
                                        rep(mpar[:, 2 * MH + g * HPG:2 * MH + (g + 1) * HPG], HD, 2), ALU.mult))
                    dve.wait_ge(*at("yg", g, t))
                    did(V.tensor_tensor(xt[:, t, o], bank_of("yg", g, t)[:, :], xt[:, t, o], ALU.add),
                        "read", "yg", g, t)
                    did(V.tensor_tensor(zs[:, t, o], xt[:, t, o], zs[:, t, o], ALU.mult), "gated", g, t)

            decays(0)
            decays(1)
            for i in range(MH // 2):
                dve.wait_ge(*at("dexp", i))
                V.tensor_tensor(ring[:, i % 3], ring[:, i % 3], rep(cb[:, i // 4, :], 2), ALU.mult).then_inc(
                    dve_done, DV.one(("gm", i)))
                if i % 4 == 0 and i:
                    finish(i // 4 - 1)
                if i + 2 < MH // 2:
                    decays(i + 2)
            finish(GROUPS - 1)
            dve.wait_ge(*at("rsqrt"))
            did(V.reciprocal(rs[:, :], rs[:, :]))
            for t in range(HALVES):
                for g in range(GROUPS):
                    o = slice(g * BANK, (g + 1) * BANK)
                    V.scalar_tensor_tensor(out=zs[:, t, o], in0=zs[:, t, o],
                                           scalar=rs[:, t * GROUPS + g:t * GROUPS + g + 1],
                                           in1=mpar[:, 3 * MH + g * BANK:3 * MH + (g + 1) * BANK], op0=ALU.mult,
                                           op1=ALU.mult).then_inc(dve_done, DV.one())

        @block.scalar
        def _(act):
            S = nc.scalar
            act.wait_ge(*at("nabs"))
            S.activation(dtv[:, :, :], dtv[:, :, :], ACT.Exp).then_inc(act_done, AC.one())
            S.activation(mpar[:, MH:2 * MH], mpar[:, MH:2 * MH], ACT.Exp).then_inc(act_done, AC.one())
            act.wait_ge(act_done, AC.n)
            S.activation(dtv[:, :, :], dtv[:, :, :], ACT.Ln, bias=1.0).then_inc(act_done, AC.one(("ln1p",)))
            for t in range(HALVES):
                for g in range(GROUPS):
                    act.wait_ge(*at("xt", t, g))
                    S.copy(xt[:, t, g * BANK:(g + 1) * BANK], bank_of("xt", t, g)[:, :]).then_inc(
                        act_done, AC.one(("read", "xt", t, g)))
            for i in range(MH // 2):
                act.wait_ge(*at("dec", i))
                S.activation(ring[:, i % 3], ring[:, i % 3], ACT.Exp).then_inc(act_done, AC.one(("dexp", i)))
            for g in range(GROUPS):
                for t in range(HALVES):
                    act.wait_ge(*at("gated", g, t))
                    if g or t:
                        act.wait_ge(act_done, AC.n)
                    S.activation(sq2[:, :], zs[:, t, g * BANK:(g + 1) * BANK], ACT.Square,
                                 accum_out=rs[:, t * GROUPS + g:t * GROUPS + g + 1]).then_inc(act_done, AC.one())
            act.wait_ge(act_done, AC.n)
            S.activation(rs[:, :], rs[:, :], ACT.Sqrt, scale=1.0 / BANK, bias=eps_n[:, 2:3]).then_inc(
                act_done, AC.one(("rsqrt",)))

        @block.tensor
        def _(pe):
            T = nc.tensor
            for t in range(HALVES):
                for g in range(GROUPS):
                    b = take(pe, "xt", t, g)
                    for c in range(4):
                        i = T.transpose(b[:, c * P:(c + 1) * P], xc[:, 4 * g + c, t * P:(t + 1) * P], C("ident"))
                    i.then_inc(pe_done, PE.one(("xt", t, g)))
            for g in range(GROUPS):
                b = take(pe, "cb", g)
                bm, cm = xc[:, DI // P + g, :], xc[:, DI // P + GROUPS + g, :]
                T.matmul(b[:, 0:SEQ], bm[:, 0:P], cm, start=True, stop=True)
                T.matmul(b[:, SEQ:BW], bm[:, P:SEQ], cm[:, P:SEQ], start=True, stop=True).then_inc(
                    pe_done, PE.one(("cb", g)))
            pe.wait_ge(*at("ad"))
            b = take(pe, "acs")
            T.matmul(b[:, 0:MH], C("upto"), ad[:, 0, :], start=True, stop=True)
            T.matmul(b[:, MH:2 * MH], C("ones"), ad[:, 0, :], start=True, stop=False)
            T.matmul(b[:, MH:2 * MH], C("upto"), ad[:, 1, :], start=False, stop=True).then_inc(
                pe_done, PE.one(("acs",)))
            pe.wait_ge(*at("read", "acs"))
            b = take(pe, "csT")
            for t in range(HALVES):
                i = T.transpose(b[0:MH, t * P:(t + 1) * P], acs[:, t, :], C("ident"))
            i.then_inc(pe_done, PE.one(("csT",)))
            pe.wait_ge(*at("read", "csT"))

            def row(i):
                b = take(pe, "row", i)
                for e in range(2):
                    m = T.matmul(b[:, e * SEQ:(e + 1) * SEQ],
                                 C("ident", MH)[:, 2 * i + e:2 * i + e + 1].to_broadcast([MH, P]), csT[:, :],
                                 start=True, stop=True)
                m.then_inc(pe_done, PE.one(("row", i)))

            row(0)
            row(1)
            for g in range(GROUPS):
                ys = [take(pe, "yg", g, t) for t in range(HALVES)]
                for k in range(4):
                    i = 4 * g + k
                    if i + 2 < MH // 2:
                        row(i + 2)
                    pe.wait_ge(*at("gm", i))
                    pe.wait_ge(*at("xdt", 1, g))
                    for e in range(2):
                        c = slice((2 * k + e) * HD, (2 * k + e + 1) * HD)
                        xo = slice(g * BANK + (2 * k + e) * HD, g * BANK + (2 * k + e + 1) * HD)
                        r = ring[:, i % 3, e, :]
                        T.matmul(ys[0][:, c], r[:, 0:P], xdt[:, 0, xo], start=True, stop=True)
                        T.matmul(ys[1][:, c], r[:, P:2 * P], xdt[:, 0, xo], start=True, stop=False)
                        m = T.matmul(ys[1][:, c], r[:, 2 * P:3 * P], xdt[:, 1, xo], start=False, stop=True)
                    m.then_inc(pe_done, PE.one(("used", i)))
                new[("yg", g, 0)] = new[("yg", g, 1)] = ("pe", PE.n)
    ssd.close()
    new[("gatedy", 0)] = new[("gatedy", 1)] = ("dve", DV.n)
    with ExitStack() as my:
        join(my, "ssm", zs, 16, a["ssm_w_out"][0], ("gatedy",))
    mam.close()

    experts(1)

    with ExitStack() as fin:
        gain_f = sb(fin, "gain_f", [P, D])
        junk_f = sb(fin, "junk_f", [P, D])
        ss_f, rstd_f = sb(fin, "ss_f", [P, HALVES]), sb(fin, "rstd_f", [P, HALVES])
        o_f = sb(fin, "o_f", [P, HALVES, D])
        new[("h", "final", 0)] = new[("h", "final", 1)] = ("dve", DV.n)
        g0 = loads["gain"]

        with nc.Block(name="final", no_gpsimd_drain=True) as block:

            @block.sync
            def _(sp):
                load(sp, "gain", gain_f[:, :], row_src("final"))
                sp.wait_ge(*at("u", "final", 1))
                load(sp, "out", a["out"][0].rearrange("(t p) d -> p t d", p=P), o_f[:, :, :])
                sp.wait_ge(*got("out"))

            @block.scalar
            def _(act):
                norm_act(act, "final", junk_f, ss_f, rstd_f)

            @block.vector
            def _(dve):
                norm_dve(dve, "final", rstd_f, o_f, gain_f, s_ld["gain"], g0 + 16)


_VECTORS = ("mu", "w0", "a0", "k_k", "k_a", "r_k")


def kernel(**inputs):
    import numpy as _np
    import concourse.bacc as _bacc
    from concourse.bass_utils import run_bass_kernel_spmd as _run

    x = {k: _np.ascontiguousarray(v) for k, v in inputs.items()}
    feat = _np.zeros((P, NFEAT), _np.float32)
    rows = _np.zeros((1, NROWS), _np.float32)

    def lay(name, v):
        o, n = FEAT[name]
        v = v.reshape(-1)
        if v.size >= P:
            feat[:, o:o + n] = v.reshape(n, P).T
        else:
            feat[0:v.size, o] = v

    mu = x["rwkv_mu"][0]
    lay("mu", mu[:3 * RW])
    lay("mu_w", mu[3 * RW:3 * RW + W_RANK])
    lay("mu_a", mu[3 * RW + W_RANK:3 * RW + W_RANK + A_RANK])
    lay("mu_g", mu[3 * RW + W_RANK + A_RANK:])
    for name, key in (("w0", "rwkv_w0"), ("a0", "rwkv_a0"), ("k_k", "rwkv_k_k"), ("k_a", "rwkv_k_a"),
                      ("r_k", "rwkv_r_k"), ("b1_k", "nsa_b1_k"), ("b1_v", "nsa_b1_v"), ("conv_w", "ssm_conv_w"),
                      ("conv_b", "ssm_conv_b")):
        lay(name, x[key][0])
    for name, v in (("mix0", x["norm_mix"][0]), ("mix1", x["norm_mix"][1]), ("ffn0", x["norm_ffn"][0]),
                    ("ffn1", x["norm_ffn"][1]), ("final", x["norm_final"]), ("gn_w", x["rwkv_gn_w"][0]),
                    ("gn_b", x["rwkv_gn_b"][0]), ("dt_bias", x["ssm_dt_bias"][0]), ("a_log", x["ssm_a_log"][0]),
                    ("d", x["ssm_d"][0]), ("ssm_norm", x["ssm_norm_w"][0]),
                    ("rb0", _np.concatenate([x["moe_bg"][0], x["moe_be"][0]])),
                    ("rb1", _np.concatenate([x["moe_bg"][1], x["moe_be"][1]]))):
        o, n = ROWS[name]
        rows[0, o:o + n] = v
    arrays = {k: x[k] for k in ("x", "hyb_w_in", "hyb_w_out", "rwkv_w_up", "rwkv_a_up", "rwkv_g_up", "nsa_w1_k",
                                "nsa_w2_k", "nsa_w1_v", "nsa_w2_v", "ssm_w_in", "ssm_w_out", "moe_w_gate",
                                "moe_w_up", "moe_w_down")}
    arrays["pe_k"] = _np.ascontiguousarray(x["nsa_pe_k"][0].T)
    arrays["pe_v"] = _np.ascontiguousarray(x["nsa_pe_v"][0].T)
    arrays["router"] = _np.ascontiguousarray(_np.concatenate([x["moe_wg"], x["moe_we"]], 2))
    arrays["feat"], arrays["rows"], arrays["tables"] = feat, rows, shape_tables()

    known = {}
    for last in (False, True):
        nc = _bacc.Bacc("TRN2", target_bir_lowering=False, num_devices=1)
        ap = {k: nc.dram_tensor(f"in_{k}", v.shape, F32, kind="ExternalInput").ap() for k, v in arrays.items()}
        ap["out"] = nc.dram_tensor("out_0", (1, SEQ, D), F32, kind="ExternalOutput").ap()
        new = {}
        build(nc, ap, known, new)
        known = new
    r = _run(nc, [{f"in_{k}": v for k, v in arrays.items()}], core_ids=[0])
    return r.results[0]["out_0"]
```
